# Optimizing a Trainium2 kernel written in Bass

```python
import math
import jax, jax.numpy as jnp
from jax import lax
import numpy as np

D_MODEL = 1024
BATCH = 1
SEQ = 512
DEPTH = 2

N_MIXERS = 4
RMS_EPS = 1e-6
LN_EPS = 1e-5

SSD_EXPAND = 2
SSD_D_INNER = SSD_EXPAND * D_MODEL
SSD_HEAD_DIM = 64
SSD_N_HEADS = SSD_D_INNER // SSD_HEAD_DIM
SSD_N_GROUPS = 8
SSD_HEADS_PER_GROUP = SSD_N_HEADS // SSD_N_GROUPS
SSD_D_STATE = 128
SSD_CONV = 4
SSD_CHUNK = 128
SSD_BC_DIM = SSD_N_GROUPS * SSD_D_STATE
SSD_CONV_DIM = SSD_D_INNER + 2 * SSD_BC_DIM
SSD_IN_DIM = SSD_D_INNER + SSD_CONV_DIM + SSD_N_HEADS

CONF_WIDTH = D_MODEL
CONF_KERNEL = 31

LRU_WIDTH = 1280
LRU_BLOCK = 256
LRU_N_BLOCKS = LRU_WIDTH // LRU_BLOCK
LRU_CONV = 4
LRU_C = 8.0

SGU_CHUNK = 128
SGU_FFN = 4 * D_MODEL
SGU_HALF = SGU_FFN // 2
SGU_GROUPS = 8
SGU_GROUP_DIM = SGU_HALF // SGU_GROUPS

FFN_HIDDEN = 2816
FFN_CONV = 3


def rms_norm(x, g):
    xf = x.astype(jnp.float32)
    y = xf * lax.rsqrt(jnp.mean(xf * xf, axis=-1, keepdims=True) + RMS_EPS)
    return (y * g.astype(jnp.float32)).astype(x.dtype)

def layer_norm(x, g, b):
    xf = x.astype(jnp.float32)
    mu = jnp.mean(xf, axis=-1, keepdims=True)
    xc = xf - mu
    y = xc * lax.rsqrt(jnp.mean(xc * xc, axis=-1, keepdims=True) + LN_EPS)
    return (y * g.astype(jnp.float32) + b.astype(jnp.float32)).astype(x.dtype)

def causal_dwconv(x, w, b):
    k, c = w.shape
    y = lax.conv_general_dilated(
        x, w[:, None, :].astype(x.dtype), window_strides=(1,), padding=[(k - 1, 0)],
        dimension_numbers=('NWC', 'WIO', 'NWC'), feature_group_count=c)
    return y + b.astype(x.dtype)

def ssd_mixer(x, in_proj, conv_w, conv_b, dt_bias, a_log, d_skip, norm_g, out_proj):
    bsz, seqlen, _ = x.shape
    f32 = jnp.float32
    nc = seqlen // SSD_CHUNK
    g, j, p, n, q = SSD_N_GROUPS, SSD_HEADS_PER_GROUP, SSD_HEAD_DIM, SSD_D_STATE, SSD_CHUNK
    zxbcdt = x @ in_proj
    z, xbc, dt = jnp.split(zxbcdt, [SSD_D_INNER, SSD_D_INNER + SSD_CONV_DIM], axis=-1)
    xbc = jax.nn.silu(causal_dwconv(xbc, conv_w, conv_b))
    xs, bm, cm = jnp.split(xbc, [SSD_D_INNER, SSD_D_INNER + SSD_BC_DIM], axis=-1)
    xs = jnp.moveaxis(xs.astype(f32).reshape(bsz, nc, q, g, j, p), 1, 0)
    bm = jnp.moveaxis(bm.astype(f32).reshape(bsz, nc, q, g, n), 1, 0)
    cm = jnp.moveaxis(cm.astype(f32).reshape(bsz, nc, q, g, n), 1, 0)
    dt = jax.nn.softplus(dt.astype(f32) + dt_bias.astype(f32))
    dt = jnp.moveaxis(dt.reshape(bsz, nc, q, g, j), 1, 0)
    a = -jnp.exp(a_log.astype(f32)).reshape(g, j)
    dsk = d_skip.astype(f32).reshape(g, j)
    causal = jnp.tril(jnp.ones((q, q), dtype=bool))[None, :, :, None, None]

    def chunk_step(state, inp):
        xc, bc, cc, dtc = inp
        acs = jnp.cumsum(dtc * a, axis=1)
        seg = acs[:, :, None] - acs[:, None, :]
        decay = jnp.exp(jnp.where(causal, seg, -jnp.inf))
        cb = jnp.einsum('btgn,bsgn->btsg', cc, bc)
        scores = cb[..., None] * decay * dtc[:, None]
        y_diag = jnp.einsum('btsgj,bsgjp->btgjp', scores, xc)
        y_off = jnp.einsum('btgn,bgjpn->btgjp', cc, state) * jnp.exp(acs)[..., None]
        decay_end = jnp.exp(acs[:, -1:] - acs) * dtc
        new_state = (state * jnp.exp(acs[:, -1])[..., None, None]
                     + jnp.einsum('bsgn,bsgj,bsgjp->bgjpn', bc, decay_end, xc))
        return new_state, y_diag + y_off + xc * dsk[..., None]

    state0 = jnp.zeros((bsz, g, j, p, n), f32)
    _, ys = lax.scan(chunk_step, state0, (xs, bm, cm, dt))
    y = jnp.moveaxis(ys, 0, 1).reshape(bsz, seqlen, SSD_D_INNER)
    y = rms_norm(y * jax.nn.silu(z.astype(f32)), norm_g)
    return y.astype(x.dtype) @ out_proj

def conformer_conv(x, pw1_w, pw1_b, dw_w, dw_b, ln_g, ln_b, pw2_w, pw2_b):
    h = jax.nn.glu(x @ pw1_w + pw1_b, axis=-1)
    h = causal_dwconv(h, dw_w, dw_b)
    h = jax.nn.silu(layer_norm(h, ln_g, ln_b))
    return h @ pw2_w + pw2_b

def rglru_block(x, in_w, in_b, conv_w, conv_b, ga_w, ga_b, gx_w, gx_b, lam, out_w, out_b):
    bsz, seqlen, _ = x.shape
    f32 = jnp.float32
    gate, xr = jnp.split(x @ in_w + in_b, 2, axis=-1)
    xr = causal_dwconv(xr, conv_w, conv_b)
    xb = xr.reshape(bsz, seqlen, LRU_N_BLOCKS, LRU_BLOCK)
    r = jax.nn.sigmoid(jnp.einsum('blhi,hij->blhj', xb, ga_w) + ga_b).reshape(bsz, seqlen, LRU_WIDTH)
    i = jax.nn.sigmoid(jnp.einsum('blhi,hij->blhj', xb, gx_w) + gx_b).reshape(bsz, seqlen, LRU_WIDTH)
    log_a = -LRU_C * r.astype(f32) * jax.nn.softplus(-lam.astype(f32))
    a = jnp.exp(log_a)
    bterm = jnp.sqrt(-jnp.expm1(2.0 * log_a)) * (i.astype(f32) * xr.astype(f32))

    def combine(lhs, rhs):
        a1, b1 = lhs
        a2, b2 = rhs
        return a1 * a2, a2 * b1 + b2

    _, h = lax.associative_scan(combine, (a, bterm), axis=1)
    y = jax.nn.gelu(gate) * h.astype(x.dtype)
    return y @ out_w + out_b

def chunked_sgu(x, in_w, in_b, ln_g, ln_b, sp_w, sp_b, out_w, out_b):
    bsz, seqlen, _ = x.shape
    nc = seqlen // SGU_CHUNK
    z = jax.nn.gelu(x @ in_w + in_b)
    u, v = jnp.split(z, 2, axis=-1)
    v = layer_norm(v, ln_g, ln_b).reshape(bsz, nc, SGU_CHUNK, SGU_GROUPS, SGU_GROUP_DIM)
    w = sp_w * jnp.tril(jnp.ones((SGU_CHUNK, SGU_CHUNK), sp_w.dtype))
    mixed = jnp.einsum('gts,bcsgk->bctgk', w, v) + jnp.swapaxes(sp_b, 0, 1)[None, None, :, :, None]
    return (u * mixed.reshape(bsz, seqlen, SGU_HALF)) @ out_w + out_b

def conv_ffn(x, up_w, conv_w, conv_b, down_w):
    h = causal_dwconv(x @ up_w, conv_w, conv_b)
    gt, val = jnp.split(h, 2, axis=-1)
    return (jax.nn.silu(gt) * val) @ down_w

def first_inputs(seed: int = 0) -> dict:
    key = jax.random.key(seed)
    keys = iter(jax.random.split(key, 64))
    f32 = jnp.float32

    def nrm(shape, scale):
        return jax.random.normal(next(keys), shape, f32) * scale

    def gain(shape):
        return 1.0 + nrm(shape, 0.02)

    def unif(shape, lo, hi):
        return jax.random.uniform(next(keys), shape, f32, minval=lo, maxval=hi)

    n_a = (DEPTH + 3) // N_MIXERS
    n_b = (DEPTH + 2) // N_MIXERS
    n_c = (DEPTH + 1) // N_MIXERS
    n_d = DEPTH // N_MIXERS
    D = D_MODEL

    x = jax.random.normal(next(keys), (BATCH, SEQ, D), f32)
    norm_mix = gain((DEPTH, D))
    norm_ffn = gain((DEPTH, D))
    norm_final = gain((D,))

    a_in_proj = nrm((n_a, D, SSD_IN_DIM), D ** -0.5)
    a_conv_w = nrm((n_a, SSD_CONV, SSD_CONV_DIM), SSD_CONV ** -0.5)
    a_conv_b = nrm((n_a, SSD_CONV_DIM), 0.02)
    dt0 = jnp.exp(unif((n_a, SSD_N_HEADS), math.log(1e-3), math.log(1e-1)))
    a_dt_bias = dt0 + jnp.log(-jnp.expm1(-dt0))
    a_log = jnp.log(unif((n_a, SSD_N_HEADS), 1.0, 16.0))
    a_d_skip = gain((n_a, SSD_N_HEADS))
    a_norm = gain((n_a, SSD_D_INNER))
    a_out_proj = nrm((n_a, SSD_D_INNER, D), SSD_D_INNER ** -0.5)

    b_pw1_w = nrm((n_b, D, 2 * CONF_WIDTH), D ** -0.5)
    b_pw1_b = nrm((n_b, 2 * CONF_WIDTH), 0.02)
    b_dw_w = nrm((n_b, CONF_KERNEL, CONF_WIDTH), CONF_KERNEL ** -0.5)
    b_dw_b = nrm((n_b, CONF_WIDTH), 0.02)
    b_ln_g = gain((n_b, CONF_WIDTH))
    b_ln_b = nrm((n_b, CONF_WIDTH), 0.02)
    b_pw2_w = nrm((n_b, CONF_WIDTH, D), CONF_WIDTH ** -0.5)
    b_pw2_b = nrm((n_b, D), 0.02)

    c_in_w = nrm((n_c, D, 2 * LRU_WIDTH), D ** -0.5)
    c_in_b = nrm((n_c, 2 * LRU_WIDTH), 0.02)
    c_conv_w = nrm((n_c, LRU_CONV, LRU_WIDTH), LRU_CONV ** -0.5)
    c_conv_b = nrm((n_c, LRU_WIDTH), 0.02)
    c_ga_w = nrm((n_c, LRU_N_BLOCKS, LRU_BLOCK, LRU_BLOCK), LRU_BLOCK ** -0.5)
    c_ga_b = nrm((n_c, LRU_N_BLOCKS, LRU_BLOCK), 0.02)
    c_gx_w = nrm((n_c, LRU_N_BLOCKS, LRU_BLOCK, LRU_BLOCK), LRU_BLOCK ** -0.5)
    c_gx_b = nrm((n_c, LRU_N_BLOCKS, LRU_BLOCK), 0.02)
    s = unif((n_c, LRU_WIDTH), 0.9, 0.999) ** (1.0 / LRU_C)
    c_lambda = jnp.log(s) - jnp.log1p(-s)
    c_out_w = nrm((n_c, LRU_WIDTH, D), LRU_WIDTH ** -0.5)
    c_out_b = nrm((n_c, D), 0.02)

    d_in_w = nrm((n_d, D, SGU_FFN), D ** -0.5)
    d_in_b = nrm((n_d, SGU_FFN), 0.02)
    d_ln_g = gain((n_d, SGU_HALF))
    d_ln_b = nrm((n_d, SGU_HALF), 0.02)
    d_sp_w = nrm((n_d, SGU_GROUPS, SGU_CHUNK, SGU_CHUNK), SGU_CHUNK ** -0.5)
    d_sp_b = gain((n_d, SGU_GROUPS, SGU_CHUNK))
    d_out_w = nrm((n_d, SGU_HALF, D), SGU_HALF ** -0.5)
    d_out_b = nrm((n_d, D), 0.02)

    f_up_w = nrm((DEPTH, D, 2 * FFN_HIDDEN), D ** -0.5)
    f_conv_w = nrm((DEPTH, FFN_CONV, 2 * FFN_HIDDEN), FFN_CONV ** -0.5)
    f_conv_b = nrm((DEPTH, 2 * FFN_HIDDEN), 0.02)
    f_down_w = nrm((DEPTH, FFN_HIDDEN, D), FFN_HIDDEN ** -0.5)

    return {'x': x, 'norm_mix': norm_mix, 'norm_ffn': norm_ffn, 'norm_final': norm_final,
            'a_in_proj': a_in_proj, 'a_conv_w': a_conv_w, 'a_conv_b': a_conv_b, 'a_dt_bias': a_dt_bias,
            'a_log': a_log, 'a_d_skip': a_d_skip, 'a_norm': a_norm, 'a_out_proj': a_out_proj,
            'b_pw1_w': b_pw1_w, 'b_pw1_b': b_pw1_b, 'b_dw_w': b_dw_w, 'b_dw_b': b_dw_b,
            'b_ln_g': b_ln_g, 'b_ln_b': b_ln_b, 'b_pw2_w': b_pw2_w, 'b_pw2_b': b_pw2_b,
            'c_in_w': c_in_w, 'c_in_b': c_in_b, 'c_conv_w': c_conv_w, 'c_conv_b': c_conv_b,
            'c_ga_w': c_ga_w, 'c_ga_b': c_ga_b, 'c_gx_w': c_gx_w, 'c_gx_b': c_gx_b,
            'c_lambda': c_lambda, 'c_out_w': c_out_w, 'c_out_b': c_out_b,
            'd_in_w': d_in_w, 'd_in_b': d_in_b, 'd_ln_g': d_ln_g, 'd_ln_b': d_ln_b,
            'd_sp_w': d_sp_w, 'd_sp_b': d_sp_b, 'd_out_w': d_out_w, 'd_out_b': d_out_b,
            'f_up_w': f_up_w, 'f_conv_w': f_conv_w, 'f_conv_b': f_conv_b, 'f_down_w': f_down_w}

def first_block(x, norm_mix, norm_ffn, norm_final,
              a_in_proj, a_conv_w, a_conv_b, a_dt_bias, a_log, a_d_skip, a_norm, a_out_proj,
              b_pw1_w, b_pw1_b, b_dw_w, b_dw_b, b_ln_g, b_ln_b, b_pw2_w, b_pw2_b,
              c_in_w, c_in_b, c_conv_w, c_conv_b, c_ga_w, c_ga_b, c_gx_w, c_gx_b, c_lambda, c_out_w, c_out_b,
              d_in_w, d_in_b, d_ln_g, d_ln_b, d_sp_w, d_sp_b, d_out_w, d_out_b,
              f_up_w, f_conv_w, f_conv_b, f_down_w):
    h = x
    for i in range(DEPTH):
        kind, j = i % N_MIXERS, i // N_MIXERS
        u = rms_norm(h, norm_mix[i])
        if kind == 0:
            m = ssd_mixer(u, a_in_proj[j], a_conv_w[j], a_conv_b[j], a_dt_bias[j], a_log[j],
                          a_d_skip[j], a_norm[j], a_out_proj[j])
        elif kind == 1:
            m = conformer_conv(u, b_pw1_w[j], b_pw1_b[j], b_dw_w[j], b_dw_b[j], b_ln_g[j], b_ln_b[j],
                               b_pw2_w[j], b_pw2_b[j])
        elif kind == 2:
            m = rglru_block(u, c_in_w[j], c_in_b[j], c_conv_w[j], c_conv_b[j], c_ga_w[j], c_ga_b[j],
                            c_gx_w[j], c_gx_b[j], c_lambda[j], c_out_w[j], c_out_b[j])
        else:
            m = chunked_sgu(u, d_in_w[j], d_in_b[j], d_ln_g[j], d_ln_b[j], d_sp_w[j], d_sp_b[j],
                            d_out_w[j], d_out_b[j])
        h = h + m
        h = h + conv_ffn(rms_norm(h, norm_ffn[i]), f_up_w[i], f_conv_w[i], f_conv_b[i], f_down_w[i])
    return rms_norm(h, norm_final)


_first_inputs = first_inputs


def first_inputs(seed=0):
    import zlib

    import numpy as np

    out = dict(_first_inputs(seed))
    spreads = {}
    factors = {'norm_ffn': 3.424,
     'norm_final': 2.994,
     'a_d_skip': 4.496,
     'a_norm': 3.487,
     'b_pw1_b': 6.364,
     'b_dw_b': 3.55,
     'b_ln_g': 6.214,
     'b_ln_b': 7.283,
     'b_pw2_b': 4.462,
     'f_conv_b': 3.551}
    for name, (base, spread) in spreads.items():
        noise = np.random.default_rng([zlib.crc32(name.encode()), seed]).standard_normal(out[name].shape)
        drawn = base * np.exp(spread * noise) if base else spread * noise
        out[name] = __import__('jax').numpy.asarray(drawn.astype(out[name].dtype))
    for name, factor in factors.items():
        out[name] = (out[name] * factor).astype(out[name].dtype)
    return out


_narrow_inputs = first_inputs


def first_inputs(seed=0):

    out = dict(_narrow_inputs(seed))
    wider = {'norm_final': 3.37, 'b_ln_g': 6.01, 'b_ln_b': 5.14, 'b_pw2_b': 6.16}
    for name, times in wider.items():
        mean = out[name].mean()
        out[name] = (mean + times * (out[name] - mean)).astype(out[name].dtype)
    return out


DEPTH_2 = 1

MEM_LEN = 256

MLA_HEADS = 8
QK_NOPE = 64
QK_ROPE = 32
V_HEAD = 64
Q_LORA = 256
KV_LORA = 256
ROPE_THETA = 10000.0
Q_BLOCK = 128

S5_GROUP_CH = 16
S5_WIDTH = 512
S5_GROUPS = S5_WIDTH // S5_GROUP_CH
S5_STATE = 64
DT_MIN = 1e-3
DT_MAX = 1e-1

XATTN_HEADS = 4
XATTN_HEAD_DIM = 128

N_EXPERTS = 64
TOP_K = 8
N_EXPERT_GROUPS = 8
TOPK_GROUPS = 4
EXPERT_FF = 256
SHARED_FF = 256
ROUTED_SCALE = 2.5
MOE_BLOCK = 128


DEEPNORM_ALPHA = (2.0 * DEPTH_2) ** 0.25
DEEPNORM_BETA = (8.0 * DEPTH_2) ** -0.25

IN_SIZES = (Q_LORA, KV_LORA, QK_ROPE, S5_WIDTH, D_MODEL, D_MODEL)
IN_WIDTH = sum(IN_SIZES)
IN_OFFSETS = tuple(int(v) for v in np.cumsum(IN_SIZES)[:-1])


def layer_norm_2(x, g, b):
    xf = x.astype(jnp.float32)
    mu = jnp.mean(xf, axis=-1, keepdims=True)
    var = jnp.mean(jnp.square(xf - mu), axis=-1, keepdims=True)
    y = (xf - mu) * lax.rsqrt(var + LN_EPS) * g.astype(jnp.float32) + b.astype(jnp.float32)
    return y.astype(x.dtype)

def rms_norm_2(x, g):
    xf = x.astype(jnp.float32)
    y = xf * lax.rsqrt(jnp.mean(jnp.square(xf), axis=-1, keepdims=True) + RMS_EPS)
    return (y * g.astype(jnp.float32)).astype(x.dtype)

def rope_cos_sin(positions):
    inv_freq = ROPE_THETA ** (-jnp.arange(0, QK_ROPE, 2, dtype=jnp.float32) / QK_ROPE)
    ang = positions.astype(jnp.float32)[..., None] * inv_freq
    return jnp.cos(ang), jnp.sin(ang)

def apply_rope(x, cos, sin):
    cos = cos.astype(x.dtype)
    sin = sin.astype(x.dtype)
    x1, x2 = jnp.split(x, 2, axis=-1)
    return jnp.concatenate([x1 * cos - x2 * sin, x2 * cos + x1 * sin], axis=-1)

def causal_block_attention(q_nope, q_rope, k_nope, k_rope, v):
    B, S, H, _ = q_nope.shape
    nb = S // Q_BLOCK
    scale = (QK_NOPE + QK_ROPE) ** -0.5
    qn_b = q_nope.reshape(B, nb, Q_BLOCK, H, QK_NOPE).transpose(1, 0, 2, 3, 4)
    qr_b = q_rope.reshape(B, nb, Q_BLOCK, H, QK_ROPE).transpose(1, 0, 2, 3, 4)
    key_pos = jnp.arange(S)

    def one_block(args):
        i, qn, qr = args
        s = (jnp.einsum('bqhd,bkhd->bhqk', qn, k_nope)
             + jnp.einsum('bqhr,bkr->bhqk', qr, k_rope)).astype(jnp.float32) * scale
        q_pos = i * Q_BLOCK + jnp.arange(Q_BLOCK)
        mask = key_pos[None, :] <= q_pos[:, None]
        s = jnp.where(mask[None, None], s, -jnp.inf)
        p = jax.nn.softmax(s, axis=-1).astype(v.dtype)
        return jnp.einsum('bhqk,bkhd->bqhd', p, v)

    out = lax.map(one_block, (jnp.arange(nb), qn_b, qr_b))
    return out.transpose(1, 0, 2, 3, 4).reshape(B, S, H, V_HEAD)

def mla_branch(h_q, h_kv, k_rope_raw, positions, q_norm_g, kv_norm_g, w_uq, w_ukv, w_mla_o):
    B, S, _ = h_q.shape
    q = (rms_norm_2(h_q, q_norm_g) @ w_uq).reshape(B, S, MLA_HEADS, QK_NOPE + QK_ROPE)
    q_nope, q_rope = q[..., :QK_NOPE], q[..., QK_NOPE:]
    kv = (rms_norm_2(h_kv, kv_norm_g) @ w_ukv).reshape(B, S, MLA_HEADS, QK_NOPE + V_HEAD)
    k_nope, v = kv[..., :QK_NOPE], kv[..., QK_NOPE:]
    cos, sin = rope_cos_sin(positions)
    q_rope = apply_rope(q_rope, cos[:, :, None, :], sin[:, :, None, :])
    k_rope = apply_rope(k_rope_raw, cos, sin)
    attn = causal_block_attention(q_nope, q_rope, k_nope, k_rope, v)
    return attn.reshape(B, S, MLA_HEADS * V_HEAD) @ w_mla_o

def _complex_affine_combine(c1, c2):
    a1r, a1i, b1r, b1i = c1
    a2r, a2i, b2r, b2i = c2
    ar = a2r * a1r - a2i * a1i
    ai = a2r * a1i + a2i * a1r
    br = a2r * b1r - a2i * b1i + b2r
    bi = a2r * b1i + a2i * b1r + b2i
    return (ar, ai, br, bi)

def s5_branch(u, a_re, a_im, log_dt, b_re, b_im, c_re, c_im, d, w_glu):
    B, S, _ = u.shape
    f32 = jnp.float32
    uf = u.astype(f32).reshape(B, S, S5_GROUPS, S5_GROUP_CH)
    dt = jnp.exp(log_dt.astype(f32))[:, None]
    ar, ai = a_re.astype(f32), a_im.astype(f32)
    mag = jnp.exp(ar * dt)
    abar_r, abar_i = mag * jnp.cos(ai * dt), mag * jnp.sin(ai * dt)
    den = ar * ar + ai * ai
    nr, ni = abar_r - 1.0, abar_i
    coef_r = ((nr * ar + ni * ai) / den)[..., None]
    coef_i = ((ni * ar - nr * ai) / den)[..., None]
    br, bi = b_re.astype(f32), b_im.astype(f32)
    bbar_r = coef_r * br - coef_i * bi
    bbar_i = coef_r * bi + coef_i * br
    bu_r = jnp.einsum('bsgh,gph->bsgp', uf, bbar_r)
    bu_i = jnp.einsum('bsgh,gph->bsgp', uf, bbar_i)
    a_r = jnp.broadcast_to(abar_r, bu_r.shape)
    a_i = jnp.broadcast_to(abar_i, bu_i.shape)
    _, _, xr, xi = lax.associative_scan(_complex_affine_combine, (a_r, a_i, bu_r, bu_i), axis=1)
    y = (jnp.einsum('bsgp,ghp->bsgh', xr, c_re.astype(f32))
         - jnp.einsum('bsgp,ghp->bsgh', xi, c_im.astype(f32)))
    y = y.reshape(B, S, S5_WIDTH) + d.astype(f32) * uf.reshape(B, S, S5_WIDTH)
    y = jax.nn.gelu(y).astype(u.dtype)
    val, gate = jnp.split(y @ w_glu, 2, axis=-1)
    return val * jax.nn.sigmoid(gate)

def hybrid_mixer(x, positions, w_in, q_norm_g, kv_norm_g, w_uq, w_ukv, w_mla_o,
                 s5_a_re, s5_a_im, s5_log_dt, s5_b_re, s5_b_im, s5_c_re, s5_c_im,
                 s5_d, w_s5_glu, w_out):
    proj = x @ w_in
    h_q, h_kv, k_rope_raw, u, g_mla, g_s5 = jnp.split(proj, IN_OFFSETS, axis=-1)
    y_mla = mla_branch(h_q, h_kv, k_rope_raw, positions, q_norm_g, kv_norm_g, w_uq, w_ukv, w_mla_o)
    y_s5 = s5_branch(u, s5_a_re, s5_a_im, s5_log_dt, s5_b_re, s5_b_im, s5_c_re, s5_c_im, s5_d, w_s5_glu)
    merged = jax.nn.sigmoid(g_mla) * y_mla + jax.nn.sigmoid(g_s5) * y_s5
    return merged @ w_out

def memory_cross_attention(x, mem, mem_ln_g, mem_ln_b, w_xq, w_xkv, w_xo):
    B, S, _ = x.shape
    M = mem.shape[1]
    m = layer_norm_2(mem, mem_ln_g, mem_ln_b)
    q = (x @ w_xq).reshape(B, S, XATTN_HEADS, XATTN_HEAD_DIM)
    kv = (m @ w_xkv).reshape(B, M, 2, XATTN_HEADS, XATTN_HEAD_DIM)
    k, v = kv[:, :, 0], kv[:, :, 1]
    s = jnp.einsum('bshd,bmhd->bhsm', q, k).astype(jnp.float32) * (XATTN_HEAD_DIM ** -0.5)
    p = jax.nn.softmax(s, axis=-1).astype(v.dtype)
    o = jnp.einsum('bhsm,bmhd->bshd', p, v).reshape(B, S, XATTN_HEADS * XATTN_HEAD_DIM)
    return o @ w_xo

def swiglu(x, w_gu, w_down):
    g, u = jnp.split(x @ w_gu, 2, axis=-1)
    return (jax.nn.silu(g) * u) @ w_down

def moe_ffn(x2d, w_router, router_bias, w_exp_gu, w_exp_down, w_sh_gu, w_sh_down):
    T, D = x2d.shape
    scores = jax.nn.sigmoid((x2d @ w_router).astype(jnp.float32))
    sel = scores + router_bias.astype(jnp.float32)
    per_group = N_EXPERTS // N_EXPERT_GROUPS
    grp_score = lax.top_k(sel.reshape(T, N_EXPERT_GROUPS, per_group), 2)[0].sum(-1)
    _, grp_idx = lax.top_k(grp_score, TOPK_GROUPS)
    grp_mask = jax.nn.one_hot(grp_idx, N_EXPERT_GROUPS, dtype=jnp.float32).sum(1) > 0
    sel = jnp.where(jnp.repeat(grp_mask, per_group, axis=1), sel, -jnp.inf)
    _, top_idx = lax.top_k(sel, TOP_K)
    w = jnp.take_along_axis(scores, top_idx, axis=1)
    w = w / jnp.sum(w, axis=-1, keepdims=True) * ROUTED_SCALE

    A = T * TOP_K
    flat_e = top_idx.reshape(A).astype(jnp.int32)
    flat_tok = jnp.repeat(jnp.arange(T, dtype=jnp.int32), TOP_K)
    flat_w = w.reshape(A).astype(x2d.dtype)
    order = jnp.argsort(flat_e)
    se = flat_e[order]
    counts = jnp.zeros((N_EXPERTS,), jnp.int32).at[flat_e].add(1)
    starts = jnp.cumsum(counts) - counts
    padded = (counts + MOE_BLOCK - 1) // MOE_BLOCK * MOE_BLOCK
    pends = jnp.cumsum(padded)
    pstarts = pends - padded
    dest = pstarts[se] + (jnp.arange(A, dtype=jnp.int32) - starts[se])
    n_blocks = (A + N_EXPERTS * (MOE_BLOCK - 1) + MOE_BLOCK - 1) // MOE_BLOCK
    P = n_blocks * MOE_BLOCK
    buf_tok = jnp.full((P,), T, jnp.int32).at[dest].set(flat_tok[order])
    buf_w = jnp.zeros((P,), x2d.dtype).at[dest].set(flat_w[order])
    block_start = jnp.arange(n_blocks, dtype=jnp.int32) * MOE_BLOCK
    block_e = jnp.minimum(jnp.searchsorted(pends, block_start, side='right'), N_EXPERTS - 1)
    x_pad = jnp.concatenate([x2d, jnp.zeros((1, D), x2d.dtype)], axis=0)

    def expert_block(args):
        tok, e = args
        return swiglu(x_pad[tok], w_exp_gu[e], w_exp_down[e])

    out = lax.map(expert_block, (buf_tok.reshape(n_blocks, MOE_BLOCK), block_e))
    out = out.reshape(P, D) * buf_w[:, None]
    routed = jnp.zeros((T + 1, D), x2d.dtype).at[buf_tok].add(out)[:T]
    return routed + swiglu(x2d, w_sh_gu, w_sh_down)

def second_inputs(seed: int = 0) -> dict:
    key = jax.random.key(seed)
    ks = iter(jax.random.split(key, 48))
    L, D = DEPTH_2, D_MODEL
    f32 = jnp.float32

    def nrm(shape, scale):
        return jax.random.normal(next(ks), shape, f32) * scale

    def gain(shape):
        return 1.0 + 0.02 * jax.random.normal(next(ks), shape, f32)

    x = jax.random.normal(next(ks), (BATCH, SEQ, D), f32)
    mem = jax.random.normal(next(ks), (BATCH, MEM_LEN, D), f32)
    positions = (jnp.arange(SEQ, dtype=jnp.int32)[None, :]
                 + jax.random.randint(next(ks), (BATCH, 1), 0, 1024, jnp.int32))
    a_re = -0.5 + 0.01 * jax.random.normal(next(ks), (L, S5_GROUPS, S5_STATE), f32)
    a_im = (jnp.pi * jnp.arange(S5_STATE, dtype=f32))[None, None, :] \
        + 0.01 * jax.random.normal(next(ks), (L, S5_GROUPS, S5_STATE), f32)
    log_dt = jax.random.uniform(next(ks), (L, S5_GROUPS), f32, math.log(DT_MIN), math.log(DT_MAX))
    beta = DEEPNORM_BETA
    return {
        "x": x,
        "mem": mem,
        "positions": positions,
        "w_in": nrm((L, D, IN_WIDTH), D ** -0.5),
        "q_norm_g": gain((L, Q_LORA)),
        "kv_norm_g": gain((L, KV_LORA)),
        "w_uq": nrm((L, Q_LORA, MLA_HEADS * (QK_NOPE + QK_ROPE)), Q_LORA ** -0.5),
        "w_ukv": nrm((L, KV_LORA, MLA_HEADS * (QK_NOPE + V_HEAD)), KV_LORA ** -0.5),
        "w_mla_o": nrm((L, MLA_HEADS * V_HEAD, D), (MLA_HEADS * V_HEAD) ** -0.5),
        "s5_a_re": a_re,
        "s5_a_im": a_im,
        "s5_log_dt": log_dt,
        "s5_b_re": nrm((L, S5_GROUPS, S5_STATE, S5_GROUP_CH), (2 * S5_GROUP_CH) ** -0.5),
        "s5_b_im": nrm((L, S5_GROUPS, S5_STATE, S5_GROUP_CH), (2 * S5_GROUP_CH) ** -0.5),
        "s5_c_re": nrm((L, S5_GROUPS, S5_GROUP_CH, S5_STATE), (2 * S5_STATE) ** -0.5 * 4.0),
        "s5_c_im": nrm((L, S5_GROUPS, S5_GROUP_CH, S5_STATE), (2 * S5_STATE) ** -0.5 * 4.0),
        "s5_d": nrm((L, S5_WIDTH), 1.0),
        "w_s5_glu": nrm((L, S5_WIDTH, 2 * D), S5_WIDTH ** -0.5),
        "w_out": nrm((L, D, D), D ** -0.5 * beta),
        "ln1_g": gain((L, D)),
        "ln1_b": nrm((L, D), 0.02),
        "mem_ln_g": gain((L, D)),
        "mem_ln_b": nrm((L, D), 0.02),
        "w_xq": nrm((L, D, XATTN_HEADS * XATTN_HEAD_DIM), D ** -0.5),
        "w_xkv": nrm((L, D, 2 * XATTN_HEADS * XATTN_HEAD_DIM), D ** -0.5),
        "w_xo": nrm((L, XATTN_HEADS * XATTN_HEAD_DIM, D), (XATTN_HEADS * XATTN_HEAD_DIM) ** -0.5 * beta),
        "ln2_g": gain((L, D)),
        "ln2_b": nrm((L, D), 0.02),
        "w_router": nrm((L, D, N_EXPERTS), D ** -0.5),
        "router_bias": nrm((L, N_EXPERTS), 0.01),
        "w_exp_gu": nrm((L, N_EXPERTS, D, 2 * EXPERT_FF), D ** -0.5),
        "w_exp_down": nrm((L, N_EXPERTS, EXPERT_FF, D), EXPERT_FF ** -0.5 * beta),
        "w_sh_gu": nrm((L, D, 2 * SHARED_FF), D ** -0.5),
        "w_sh_down": nrm((L, SHARED_FF, D), SHARED_FF ** -0.5 * beta),
        "ln3_g": gain((L, D)),
        "ln3_b": nrm((L, D), 0.02),
    }

def second_block(x, mem, positions, w_in, q_norm_g, kv_norm_g, w_uq, w_ukv, w_mla_o,
              s5_a_re, s5_a_im, s5_log_dt, s5_b_re, s5_b_im, s5_c_re, s5_c_im, s5_d,
              w_s5_glu, w_out, ln1_g, ln1_b, mem_ln_g, mem_ln_b, w_xq, w_xkv, w_xo,
              ln2_g, ln2_b, w_router, router_bias, w_exp_gu, w_exp_down, w_sh_gu,
              w_sh_down, ln3_g, ln3_b):
    B, S, D = x.shape
    for l in range(DEPTH_2):
        mix = hybrid_mixer(x, positions, w_in[l], q_norm_g[l], kv_norm_g[l], w_uq[l], w_ukv[l],
                           w_mla_o[l], s5_a_re[l], s5_a_im[l], s5_log_dt[l], s5_b_re[l],
                           s5_b_im[l], s5_c_re[l], s5_c_im[l], s5_d[l], w_s5_glu[l], w_out[l])
        x = layer_norm_2(DEEPNORM_ALPHA * x + mix, ln1_g[l], ln1_b[l])
        xa = memory_cross_attention(x, mem, mem_ln_g[l], mem_ln_b[l], w_xq[l], w_xkv[l], w_xo[l])
        x = layer_norm_2(DEEPNORM_ALPHA * x + xa, ln2_g[l], ln2_b[l])
        ff = moe_ffn(x.reshape(B * S, D), w_router[l], router_bias[l], w_exp_gu[l],
                     w_exp_down[l], w_sh_gu[l], w_sh_down[l]).reshape(B, S, D)
        x = layer_norm_2(DEEPNORM_ALPHA * x + ff, ln3_g[l], ln3_b[l])
    return x


_first_inputs_2 = second_inputs


def second_inputs(seed=0):
    import zlib

    import numpy as np

    out = dict(_first_inputs_2(seed))
    spreads = {}
    factors = {'q_norm_g': 8.0,
     'kv_norm_g': 8.0,
     's5_a_re': 8.0,
     'mem_ln_g': 7.491,
     'ln3_g': 2.851,
     'ln3_b': 2.942}
    for name, (base, spread) in spreads.items():
        noise = np.random.default_rng([zlib.crc32(name.encode()), seed]).standard_normal(out[name].shape)
        drawn = base * np.exp(spread * noise) if base else spread * noise
        out[name] = __import__('jax').numpy.asarray(drawn.astype(out[name].dtype))
    for name, factor in factors.items():
        out[name] = (out[name] * factor).astype(out[name].dtype)
    return out


_narrow_inputs_2 = second_inputs


def second_inputs(seed=0):
    out = dict(_narrow_inputs_2(seed))
    wider = {'s5_a_re': 12.0, 'mem_ln_b': 4.76, 'ln3_g': 3.21, 'ln3_b': 3.21}
    for name, times in wider.items():
        mean = out[name].mean()
        out[name] = (mean + times * (out[name] - mean)).astype(out[name].dtype)
    return out


def setup_inputs(seed=0):
    out = dict(first_inputs(seed))
    for name, value in second_inputs(seed + 1).items():
        if name != "x":
            out[name + "_2"] = value
    return out


def reference(
    x, norm_mix, norm_ffn, norm_final, a_in_proj, a_conv_w, a_conv_b, a_dt_bias, a_log,
    a_d_skip, a_norm, a_out_proj, b_pw1_w, b_pw1_b, b_dw_w, b_dw_b, b_ln_g, b_ln_b, b_pw2_w,
    b_pw2_b, c_in_w, c_in_b, c_conv_w, c_conv_b, c_ga_w, c_ga_b, c_gx_w, c_gx_b, c_lambda,
    c_out_w, c_out_b, d_in_w, d_in_b, d_ln_g, d_ln_b, d_sp_w, d_sp_b, d_out_w, d_out_b, f_up_w,
    f_conv_w, f_conv_b, f_down_w, mem_2, positions_2, w_in_2, q_norm_g_2, kv_norm_g_2, w_uq_2,
    w_ukv_2, w_mla_o_2, s5_a_re_2, s5_a_im_2, s5_log_dt_2, s5_b_re_2, s5_b_im_2, s5_c_re_2,
    s5_c_im_2, s5_d_2, w_s5_glu_2, w_out_2, ln1_g_2, ln1_b_2, mem_ln_g_2, mem_ln_b_2, w_xq_2,
    w_xkv_2, w_xo_2, ln2_g_2, ln2_b_2, w_router_2, router_bias_2, w_exp_gu_2, w_exp_down_2,
    w_sh_gu_2, w_sh_down_2, ln3_g_2, ln3_b_2,
):
    x = first_block(
        x, norm_mix, norm_ffn, norm_final, a_in_proj, a_conv_w, a_conv_b, a_dt_bias, a_log,
        a_d_skip, a_norm, a_out_proj, b_pw1_w, b_pw1_b, b_dw_w, b_dw_b, b_ln_g, b_ln_b, b_pw2_w,
        b_pw2_b, c_in_w, c_in_b, c_conv_w, c_conv_b, c_ga_w, c_ga_b, c_gx_w, c_gx_b, c_lambda,
        c_out_w, c_out_b, d_in_w, d_in_b, d_ln_g, d_ln_b, d_sp_w, d_sp_b, d_out_w, d_out_b,
        f_up_w, f_conv_w, f_conv_b, f_down_w,
    )
    return second_block(
        x, mem_2, positions_2, w_in_2, q_norm_g_2, kv_norm_g_2, w_uq_2, w_ukv_2, w_mla_o_2,
        s5_a_re_2, s5_a_im_2, s5_log_dt_2, s5_b_re_2, s5_b_im_2, s5_c_re_2, s5_c_im_2, s5_d_2,
        w_s5_glu_2, w_out_2, ln1_g_2, ln1_b_2, mem_ln_g_2, mem_ln_b_2, w_xq_2, w_xkv_2, w_xo_2,
        ln2_g_2, ln2_b_2, w_router_2, router_bias_2, w_exp_gu_2, w_exp_down_2, w_sh_gu_2,
        w_sh_down_2, ln3_g_2, ln3_b_2,
    )


_drawn_inputs = setup_inputs


def setup_inputs(seed=0):
    import zlib

    import numpy as np

    out = dict(_drawn_inputs(seed))
    spreads = {}
    factors = {}
    for name, (base, spread) in spreads.items():
        noise = np.random.default_rng([zlib.crc32(name.encode()), seed]).standard_normal(out[name].shape)
        drawn = base * np.exp(spread * noise) if base else spread * noise
        out[name] = __import__('jax').numpy.asarray(drawn.astype(out[name].dtype))
    for name, factor in factors.items():
        out[name] = (out[name] * factor).astype(out[name].dtype)
    return out
```

```python
from contextlib import ExitStack

import numpy as np

import concourse.bass as bass
from concourse import mybir

F32 = mybir.dt.float32
F32R = mybir.dt.float32r
BF16 = mybir.dt.bfloat16
I32 = mybir.dt.int32
ALU = mybir.AluOpType
ACT = mybir.ActivationFunctionType
AX = mybir.AxisListType

P = 128
T = 512
D = 1024
NK = D // P
TC = T // P
NSLOT = 2
NBANK = 4
SLOT = 8 * 512
PAD = 3

D_INNER, HEADS, CONV_DIM = 2048, 32, 4096
FFN, FFN_TILES = 2816, 22
CONF_TAPS = 31
ROUND = 12582912.0
TWO_PI_HI = 6.28125
TWO_PI_LO = 2.0 * np.pi - TWO_PI_HI
TWO_PI = float(2.0 * np.pi)
TWO_PI_DOWN = 6.283185
PI_BELOW = 3.1415925
RMS_EPS, LN_EPS = 1e-6, 1e-5


class Count:

    def __init__(self, start=0):
        self.s, self.dyn, self.per, self.s0 = start, 0, 0, 0

    @property
    def v(self):
        return self.s + self.dyn

    def inc(self, k=1):
        self.s += k

    def enter(self, i, per):
        self.s0, self.per, self.dyn = self.s, per, i * per

    def leave(self, n):
        assert self.s - self.s0 == self.per, (self.s - self.s0, self.per)
        self.s, self.dyn = self.s0 + n * self.per, 0


def at(ap, i):
    return ap[:, i, :] if isinstance(i, int) else ap[:, bass.ds(i, 1), :].squeeze(1)


def col(ap, i):
    return ap[:, i:i + 1] if isinstance(i, int) else ap[:, bass.ds(i, 1)]


def cols(ap, i, n):
    return ap[:, i:i + n] if isinstance(i, int) else ap[:, bass.ds(i, n)]


class Params:

    def __init__(self):
        self.rows, self.base, self.n = [], {}, 0

    def add(self, name, ap):
        n = ap.shape[0]
        self.base[name] = self.n
        done = 0
        while done < n:
            k = min(n - done, P - (self.n % P))
            self.rows.append((self.n // P, self.n % P, k, ap[done:done + k, :]))
            done += k
            self.n += k

    @property
    def blocks(self):
        return -(-self.n // P)


def halves(k, n):
    cut = -(-k // 2) * n
    return (0, cut), (cut, k * n)


def rows_of(ap):
    return ap.rearrange("(n p) -> n p", p=P)


UNUSED = ("c_in_w", "c_in_b", "c_conv_w", "c_conv_b", "c_ga_w", "c_ga_b", "c_gx_w", "c_gx_b", "c_lambda", "c_out_w",
          "c_out_b", "d_in_w", "d_in_b", "d_ln_g", "d_ln_b", "d_sp_w", "d_sp_b", "d_out_w", "d_out_b")


def shape_constants():
    k = np.zeros((P, 68), np.float32)
    inv = (np.float32(10000.0) ** (-np.arange(0, 32, 2, dtype=np.float32) / np.float32(32))).astype(np.float32)
    k[64:96, 0] = np.concatenate([inv, inv])
    k[64:96, 1] = np.concatenate([-np.ones(16, np.float32), np.ones(16, np.float32)])
    k[:, 2] = (np.arange(P) // 16) % 2 == 0
    k[:, 3] = (np.arange(P) // 16) % 2 == 1
    k[:, 4:] = (np.arange(8)[:, None] > np.arange(8)[None, :]).reshape(64)
    return {"shape_constants": k}


def build(nc, A, out):
    ctx = ExitStack()
    with ctx:
        def sb(name, shape, dt=F32):
            return ctx.enter_context(nc.sbuf_tensor(name, shape, dt))

        def sb2(name, shape):
            with nc.sbuf_tensor(name + "_r", shape, F32R) as r:
                pass
            return sb(name, shape), r

        def sem(name):
            return ctx.enter_context(nc.semaphore(name))

        par = Params()
        par.add("norm_mix", A["norm_mix"].rearrange("l (n p) -> (l n) p", p=P))
        par.add("norm_ffn", A["norm_ffn"].rearrange("l (n p) -> (l n) p", p=P))
        par.add("norm_final", rows_of(A["norm_final"]))
        par.add("a_conv_w", A["a_conv_w"][0].rearrange("k (n p) -> (k n) p", p=P))
        par.add("a_conv_b", rows_of(A["a_conv_b"][0]))
        par.add("a_norm", rows_of(A["a_norm"][0]))
        par.add("f_conv_w", A["f_conv_w"].rearrange("l k (n p) -> (l k n) p", p=P))
        par.add("f_conv_b", A["f_conv_b"].rearrange("l (n p) -> (l n) p", p=P))
        par.add("pw1_b", rows_of(A["b_pw1_b"][0]))
        par.add("dw_w", A["b_dw_w"][0].rearrange("k (n p) -> (k n) p", p=P))
        for name in ("dw_b", "ln_g", "ln_b", "pw2_b"):
            par.add(name, rows_of(A["b_" + name][0]))
        for name in ("q_norm_g", "kv_norm_g", "s5_d", "ln1_g", "ln1_b", "mem_ln_g", "mem_ln_b", "ln2_g", "ln2_b"):
            par.add(name, rows_of(A[name + "_2"][0]))
        for name in ("s5_a_re", "s5_a_im"):
            par.add(name, A[name + "_2"][0].rearrange("(n two) p -> n (two p)", two=2))
        NPB = par.blocks
        NPB_TILES = -(-NPB // 4)

        ident = sb("ident", [P, P])
        ones = sb("ones", [P, P])
        tri = sb("tri", [P, P])
        stri = sb("stri", [P, P])
        kc = sb("kc", [P, 4])
        pcol = sb("pcol", [P, NPB * P])
        hT = sb("hT", [P, NK, T])
        uT, uT_r = sb2("uT", [P, NK, T])
        sq, sq_r = sb2("sq", [P, NK, T])
        wring, wlo = zip(*[sb2(f"wring{r}", [P, SLOT]) for r in range(NSLOT)])
        raw = [sb(f"raw{r}", [P, PAD + T]) for r in range(NBANK)]
        std = sb("std", [P, T])
        rinv = sb("rinv", [P, T])
        ARENA = 27900
        arena, arena_r = sb2("arena", [P, ARENA])

        top = [0]

        def carve(*shape, dt=F32, at_=None):
            n = int(np.prod(shape))
            if dt == BF16:
                n = (n + 1) // 2
            a = top[0]
            top[0] += n
            assert top[0] <= ARENA, (top[0], ARENA)
            ap = arena[:, a:a + n]
            if dt != F32:
                ap = ap.bitcast(dt)
            if len(shape) == 2:
                ap = ap.rearrange("p (a b) -> p a b", b=shape[1])
            elif len(shape) == 3:
                ap = ap.rearrange("p (a b c) -> p a b c", b=shape[1], c=shape[2])
            return ap

        def carve_r(*shape):
            a = top[0]
            ap = carve(*shape)
            r = arena_r[:, a:top[0]]
            return ap, r if len(shape) == 1 else r.rearrange("p (a b) -> p a b", b=shape[1])

        def pcols(name, i, n=1):
            return cols(pcol, par.base[name] + i, n)

        def pc(name, i=0):
            return col(pcol, par.base[name] + i)

        tp = [ctx.enter_context(nc.psum_tensor(f"tp{i}", [P, T], F32)) for i in range(NBANK)]
        mp = [ctx.enter_context(nc.psum_tensor(f"mp{i}", [P, T], F32)) for i in range(4)]

        w_ready = [sem(f"w_ready{r}") for r in range(NSLOT)]
        tile_done = sem("tile_done")
        tile_evac = sem("tile_evac")
        done = {e: sem(f"{e}_done") for e in ("pe", "act", "dve", "pool")}
        param_in = sem("param_in")
        x_in = sem("x_in")
        misc_in = sem("misc_in")
        consts_ready = sem("consts_ready")
        sq_ready = sem("sq_ready")
        stat_ready = sem("stat_ready")
        std_ready = sem("std_ready")
        xc_ready = sem("xc_ready")
        ln_ready = sem("ln_ready")
        dve_chain = sem("dve_chain")
        act_chain = sem("act_chain")
        pool_chain = sem("pool_chain")
        conv_ready = sem("conv_ready")
        whi_ready = sem("whi_ready")
        wlo_ready = sem("wlo_ready")
        xhi_ready = sem("xhi_ready")
        xlo_ready = sem("xlo_ready")
        silu_ready = sem("silu_ready")
        out_sem = sem("out_sem")

        pk = carve(NPB, P)
        xtok = carve(TC, D)
        top[0] = 0
        acc = [carve(T) for _ in range(NBANK)]
        yT = carve(16, T)
        xg = [carve(2, T) for _ in range(2)]
        bg = [carve(T) for _ in range(2)]
        cg = [carve(T) for _ in range(2)]
        xtk = carve(TC, 256)
        btk = carve(TC, P)
        cbm = carve(TC, P)
        xdt = carve(TC, 256)
        xde = carve(TC, 256)
        ea = [carve(T) for _ in range(4)]
        sg = [carve(T) for _ in range(4)]
        cts = carve(4, T)
        st = [carve(256) for _ in range(3)]
        acsm = [carve(T) for _ in range(2)]
        acsT = carve(T)
        dtb = carve(HEADS)
        alog = carve(HEADS)
        dskc = carve(16)
        wdt = carve(NK, HEADS)
        dtx = carve(TC * HEADS)
        dtk = carve(TC * HEADS)
        dA = carve(TC * HEADS)
        acs = carve(TC * HEADS)
        dend = carve(TC * HEADS)
        top[0] = ARENA - NSLOT * SLOT
        flat = lambda b: b[:].rearrange("p a b -> p (a b)")
        whi = [carve_r(SLOT) for _ in range(NSLOT)]
        wdhi = [(flat(uT), flat(uT_r)), (flat(sq), flat(sq_r))]
        u_lo, u_hi = (uT, uT_r), (sq, sq_r)
        h_lo = (hT, uT_r)
        top[0] = NBANK * T + 16 * T
        yhi = carve_r(16, T)
        top[0] = NBANK * T
        y_lo = carve_r(16, T)
        top[0] = NBANK * T
        ffa = carve(FFN_TILES, T)
        sgate = [carve(T) for _ in range(2)]
        ffhi = carve_r(FFN_TILES, T)
        top[0] = NBANK * T
        ff_lo = carve_r(FFN_TILES, T)
        top[0] = NBANK * T
        hg = carve(NK, T + CONF_TAPS - 1)
        glu_a = [carve(T) for _ in range(2)]
        glu_b = [carve(T) for _ in range(2)]
        cv = carve(NK, T)
        xc = sq
        lnsq = carve(NK, T)

        top[0] = NBANK * T
        gm, gm_r = carve_r(NK, T)
        gs = carve(NK, T)
        hq = carve(2, T)
        hkv = carve(2, T)
        us, us_r = carve_r(4, T)
        cosT = carve(T)
        sinT = carve(T)
        kro = carve(T)
        krr = carve(T)
        sc_consts = carve(4 + 64)
        second_top = top[0]
        posi = carve(T, dt=I32)
        ang = carve(T)
        turns = carve(T)
        wkr = carve(NK, 64)
        assert top[0] <= ARENA - NSLOT * SLOT
        top[0] = second_top
        attnT = carve(4, T)
        qh = [carve(T) for _ in range(2)]
        kh = [carve(T) for _ in range(2)]
        vh = [carve(TC, 64) for _ in range(2)]
        rq = carve(T)
        pb = [carve(T) for _ in range(3)]
        pt = [carve(T) for _ in range(2)]
        smax = carve(32)
        nmax = carve(32)
        rsum = carve(32)
        rrec = carve(32)
        negm = carve(P)
        wuq = uT[:, 0:3, :].rearrange("p a b -> p (a b)").rearrange("p (k n) -> p k n", n=768)
        wrot = uT[:, 3, :].rearrange("p (k h n) -> p k h n", k=2, n=32)
        wukv = uT[:, 4:8, :].rearrange("p a b -> p (a b)").rearrange("p (k n) -> p k n", n=1024)
        S5T = 16
        top[0] = second_top
        s5p = carve(20, S5T)
        ldt = carve(S5T)
        bre = carve(S5T, 16)
        bim = carve(S5T, 16)
        bda = carve(S5T, 32)
        bdb = carve(S5T, 32)
        btmp = carve(S5T, 16)
        btr = carve(4, P)
        bti = carve(4, P)
        iot = carve(T)
        y5 = carve(T)
        t5 = carve(T)
        zr = [carve(T) for _ in range(2)]
        zi = [carve(T) for _ in range(2)]
        cbig = sq[:, 0:2, :].rearrange("p a (b c) -> p a b c", c=P)
        ctr = sq[:, 2, :].rearrange("p (a b) -> p a b", b=P)
        ctn = sq[:, 3, :].rearrange("p (a b) -> p a b", b=P)
        cti = sq[:, 4, :].rearrange("p (a b) -> p a b", b=P)
        craw = sq[:, 5, :].rearrange("p (two a b) -> p two a b", two=2, b=64)
        wtb = [sq[:, 6 + k, :] for k in range(2)]
        ct5 = [uT[:, k, :] for k in range(2)]
        st5 = [uT[:, 2 + k, :] for k in range(2)]
        pr5 = [uT[:, 4 + k, :] for k in range(4)]
        top[0] = ARENA - 4 * T
        us_hi, us_lo = carve_r(4, T), (us, us_r)
        top[0] = ARENA - NK * T
        gm_hi, gm_lo = carve_r(NK, T), (gm, gm_r)
        top[0] = NBANK * T
        memk = carve(2, D)
        memT = carve(NK, 256)
        memc = carve(NK, 256)
        memq = carve(NK, 256)
        mT = carve(NK, 256)
        qx = carve(4, T)
        kx = carve(4, 256)
        vx = carve(2, T)
        ox = carve(4, T)
        xpb = [carve(256) for _ in range(3)]
        xpt = [carve(256) for _ in range(2)]
        xsm = [carve(16) for _ in range(4)]
        NE, CAP, NTOK = 64, P, T
        CONVS = 32 + 16 + 8 + 2 * (2 * FFN_TILES + 8) + 8 + 8 + 8 + 8 + 8 + (2 + 8)
        TOK_TILES = (NPB_TILES + NK + 32 + 16 + 8 + 2 * (2 * FFN_TILES + 8) + 16 + 8 + 26 + 32 + 8 + 5 + 32 + 16 + 8
                     + NK + 10 + 8)
        RES_TILES = TOK_TILES + 8 + (4 + 8)
        top[0] = 0
        wgu = (wring[0], wring[1], flat(uT), flat(sq))
        wdn = [carve(2, D) for _ in range(4)]
        xe = [carve(D) for _ in range(2)]
        xeT = [carve(NK, P) for _ in range(2)]
        ye = [carve(D) for _ in range(2)]
        oneh = [carve(4, P) for _ in range(2)]
        silg = carve(256)
        actE = carve(256)
        actET = carve(2, P)
        sidx = [carve(1, dt=I32) for _ in range(4)]
        swt = [carve(1) for _ in range(4)]
        sidf = carve(2)
        slotrow = carve(P)
        slotcol = carve(2)
        posm = carve(TC, NE)
        rinfo = carve(TC * NE, 3)
        scr = carve(TC * NE)
        sel = carve(TC * NE)
        mask = carve(TC * NE)
        rtmp = carve(TC * NE)
        m8 = carve(TC * 8, 8)
        gsc = carve(TC, 8)
        gmask = carve(TC, 8)
        gpair = carve(TC * 8, 8)
        geq = carve(TC * 8, 8)
        rden = carve(TC)
        rbias = carve(NE)
        wrt = carve(NK, NE)
        cntf = carve(1)
        cnti = carve(1, dt=I32)
        sc_c2 = carve(4 + 64)
        tokb = [carve(D) for _ in range(2)]
        sact = carve(2, T)
        ssil = [carve(T) for _ in range(2)]
        zrow = carve(D)
        top[0] = 0
        fin = [carve(D) for _ in range(4)]
        g3 = carve(D)
        b3 = carve(D)
        bst = carve(4 * 2, 6)
        mv = carve(4, 2)
        rs3 = carve(4)
        top[0] = 0

        xtab = nc.dram_tensor("xtab", (NTOK + P, D), F32).ap()
        ytab = nc.dram_tensor("ytab", (NTOK + P, D), F32).ap()
        ALPHA = float(2.0 ** 0.25)
        MLA_SCALE = float(96 ** -0.5)
        X_SCALE = float(128 ** -0.5)
        att = [{k: sem(f"{n}_{k}") for k in ("scores", "masked", "exped", "normed", "turned", "evac", "pv", "out")}
               for n in ("mla", "xatt")]
        heads_in = sem("heads_in")
        in2 = sem("in2")
        in3 = sem("in3")
        ang_ready = sem("ang_ready")
        sin_ready = sem("sin_ready")
        head_q = sem("head_q")
        s5_a, s5_b, s5_c = sem("s5_tables"), sem("s5_rotated"), sem("s5_products")
        s5_ph, s5_yd = sem("s5_phases"), sem("s5_y_done")
        s5_cat = sem("s5_params")
        rt = {k: sem(f"router_{k}") for k in ("logits", "scores", "mask", "pos")}
        tok_out = sem("tok_out")

        wg_ready = [sem(f"wg_ready{b}") for b in range(4)]
        wd_ready = [sem(f"wd_ready{b}") for b in range(4)]
        moe = {k: sem(f"moe_{k}") for k in (
            "onehot",
            "idx",
            "conv",
            "turned",
            "xT",
            "gu",
            "silu",
            "act",
            "actturned",
            "actT",
            "down",
            "y0", "y1",
            "scattered",
        )}
        gathered = [sem(f"gathered{b}") for b in range(2)]
        fin_in = sem("fin_in")
        fin_ready = sem("fin_ready")
        var_ready, rs_ready = sem("var_ready"), sem("rs_ready")
        wait_taken = sem("wait_taken")
        moe_row = sem("moe_row")
        moe_again = sem("moe_again")
        block = ctx.enter_context(nc.Block())
        GPER = {"pe": 13, "act": 15, "dve": 20}
        core = {e: sem(f"ssd_core_{e}") for e in GPER}
        ysq_used = sem("ysq_used")
        glu_ready = sem("glu_ready")
        negabs_ready = sem("negabs_ready")
        softplus_ready = sem("softplus_ready")
        dA_ready = sem("dA_ready")
        dend_ready = sem("dend_ready")

        def phase_end(eng, me, ph):
            ph.inc()
            eng.drain().then_inc(done[me], 1)
            for other in done:
                if other != me:
                    eng.wait_ge(done[other], ph.v)

        @block.sync
        def _(sp):
            tiles = Count()
            state = {"slots": 0, "last": 0}

            def slot(n_tiles, parts):
                r = state["slots"] % NSLOT
                if state["slots"] >= NSLOT:
                    sp.wait_ge(tile_done, tiles.v - state["last"])
                for dst, src in parts(wring[r]):
                    sp.dma_start(dst, src).then_inc(w_ready[r], 16)
                state["slots"] += 1
                state["last"] = n_tiles
                tiles.inc(n_tiles)

            def loop(n, slots_per, tiles_per, body):
                sp.wait_ge(tile_done, tiles.s - state["last"])
                state["last"] = tiles_per // slots_per
                s0 = state["slots"]
                with sp.Fori(0, n) as i:
                    tiles.enter(i, tiles_per)
                    body(i)
                tiles.leave(n)
                state["slots"] = s0 + n * slots_per

            def thirds(w, k, c0, n):
                def parts(ring):
                    dst = ring[:, 0:k * n].rearrange("p (k n) -> p k n", n=n)
                    src = w.rearrange("(k p) n -> p k n", p=P)
                    src = src[:, :, c0:c0 + n] if isinstance(c0, int) else src[:, :, bass.ds(c0, n)]
                    cuts = [0, -(-k // 3), k - k // 3, k]
                    return [(dst[:, a:b, :], src[:, a:b, :]) for a, b in zip(cuts, cuts[1:])]
                return parts

            def two_cols(w, c0, c1, n):
                def parts(ring):
                    dst = ring[:, 0:8 * 2 * n].rearrange("p (k n) -> p k n", n=2 * n)
                    src = w.rearrange("(k p) n -> p k n", p=P)
                    run = lambda c: src[:, :, c:c + n] if isinstance(c, int) else src[:, :, bass.ds(c, n)]
                    second = run(c1)
                    return [(dst[:, :, 0:n], run(c0)), (dst[:, 0:4, n:2 * n], second[:, 0:4, :]),
                            (dst[:, 4:8, n:2 * n], second[:, 4:8, :])]
                return parts

            def group_cols(w, g):
                def parts(ring):
                    dst = ring[:, :].rearrange("p (k n) -> p k n", n=512)
                    src = w.rearrange("(k p) n -> p k n", p=P)
                    x0 = D_INNER + g * 256
                    x = src[:, :, x0:x0 + 256] if isinstance(g, int) else src[:, :, bass.ds(x0, 256)]
                    one = lambda c: src[:, :, c:c + P] if isinstance(g, int) else src[:, :, bass.ds(c, P)]
                    b0 = 2 * D_INNER + g * P
                    return [(dst[:, :, 0:256], x), (dst[:, :, 256:384], one(b0)), (dst[:, :, 384:512], one(b0 + 1024))]
                return parts

            sp.dma_start(xtok, A["x"][0].rearrange("(c p) d -> p c d", p=P)).then_inc(x_in, 16)
            for b, r0, n, src in par.rows:
                sp.dma_start(pk[r0:r0 + n, b, :], src).then_inc(param_in, 16)
            tiles.inc(NPB_TILES + NK)
            for e in done:
                sp.wait_ge(done[e], 1)
            sp.dma_start(dtb, A["a_dt_bias"][0].partition_broadcast(P)).then_inc(misc_in, 16)
            sp.dma_start(alog, A["a_log"][0].partition_broadcast(P)).then_inc(misc_in, 16)
            dsk = A["a_d_skip"][0].rearrange("(t two) -> two t", two=2)
            for k in range(2):
                sp.dma_start(dskc[64 * k:64 * k + 64, :], dsk[k, :].partition_broadcast(64), allow_slow_non_contiguous=True).then_inc(misc_in, 16)
            w_in = A["a_in_proj"][0]
            sp.dma_start(wdt, w_in[:, D_INNER + CONV_DIM:].rearrange("(k p) n -> p k n", p=P)).then_inc(misc_in, 16)

            def gslot(g):
                slot(4, group_cols(w_in, g))

            gslot(0)
            gslot(1)

            def body(i):
                gslot(2 * i + 2)
                gslot(2 * i + 3)
            loop(3, 2, 8, body)
            for s in range(4):
                slot(4, thirds(w_in, 8, 512 * s, 512))
            for s in range(4):
                slot(2, thirds(A["a_out_proj"][0], 16, 256 * s, 256))

            def ffn(layer):
                up, down = A["f_up_w"][layer], A["f_down_w"][layer]

                def body(i):
                    for j in range(2):
                        slot(4, two_cols(up, (2 * i + j) * 256, FFN + (2 * i + j) * 256, 256))
                loop(5, 2, 8, body)
                slot(4, two_cols(up, 10 * 256, FFN + 10 * 256, 256))

                def body2(i):
                    for j in range(2):
                        slot(1, thirds(down, FFN_TILES, (2 * i + j) * P, P))
                loop(4, 2, 2, body2)

            ffn(0)
            for s in range(4):
                slot(4, two_cols(A["b_pw1_w"][0], 256 * s, D + 256 * s, 256))
            for s in range(2):
                slot(4, thirds(A["b_pw2_w"][0], 8, 512 * s, 512))
            ffn(1)
            w2 = A["w_in_2"][0]
            for e in done:
                sp.wait_ge(done[e], 17)
            w2p = w2.rearrange("(k p) n -> p k n", p=P)
            sp.dma_start(wkr[:, :, 0:32], w2p[:, :, 512:544]).then_inc(in2, 16)
            sp.dma_start(wkr[:, :, 32:48], w2p[:, :, 528:544]).then_inc(in2, 16)
            sp.dma_start(wkr[:, :, 48:64], w2p[:, :, 512:528]).then_inc(in2, 16)
            sp.dma_start(posi[64:96, :], A["positions_2"][0].partition_broadcast(32)).then_inc(in2, 16)
            sp.dma_start(sc_consts, A["shape_constants"]).then_inc(in2, 16)
            slot(4, thirds(w2, 8, 0, 512))
            tiles.inc(2)
            for s in range(5):
                slot(4, thirds(w2, 8, 544 + 512 * s, 512))
            tiles.inc(4 * 8)
            for e in done:
                sp.wait_ge(done[e], 19)
            sp.dma_start(wuq, A["w_uq_2"][0].rearrange("(k p) n -> p k n", p=P)).then_inc(heads_in, 16)
            sp.dma_start(wukv, A["w_ukv_2"][0].rearrange("(k p) n -> p k n", p=P)).then_inc(heads_in, 16)
            for k in range(2):
                heads = A["w_uq_2"][0][k * P:(k + 1) * P, :].rearrange("p (h n) -> p h n", n=96)
                sp.dma_start(wrot[:, k, :, 0:16], heads[:, :, 80:96]).then_inc(heads_in, 16)
                sp.dma_start(wrot[:, k, :, 16:32], heads[:, :, 64:80]).then_inc(heads_in, 16)

            def quarter(w, k, c0, n):
                def parts(ring):
                    dst = ring[:, 0:k * n].rearrange("p (k n) -> p k n", n=n)
                    src = w.rearrange("(k p) n -> p k n", p=P)[:, :, c0:c0 + n]
                    cuts = [0, n // 4, n // 2, n]
                    return [(dst[:, :, a:b], src[:, :, a:b]) for a, b in zip(cuts, cuts[1:])]
                return parts

            def glu_cols(w, c0, c1, n):
                def parts(ring):
                    dst = ring[:, :].rearrange("p (k n) -> p k n", n=2 * n)
                    src = w.rearrange("(k p) n -> p k n", p=P)
                    h = n // 2
                    return [(dst[:, :, 0:n], src[:, :, c0:c0 + n]), (dst[:, :, n:n + h], src[:, :, c1:c1 + h]),
                            (dst[:, :, n + h:2 * n], src[:, :, c1 + h:c1 + n])]
                return parts

            slot(8, quarter(A["w_mla_o_2"][0], 4, 0, 1024))
            for e in done:
                sp.wait_ge(done[e], 23)
            for two in range(2):
                half = slice(64 * two, 64 * two + 64)
                ld = A["s5_log_dt_2"][0].rearrange("(j two) -> two j", two=2)
                sp.dma_start(ldt[half, :], ld[two, :].partition_broadcast(64), allow_slow_non_contiguous=True).then_inc(in3, 16)
                for dst, name in ((bre, "s5_b_re_2"), (bim, "s5_b_im_2")):
                    v = A[name][0].rearrange("(j two) p h -> two p j h", two=2)
                    sp.dma_start(dst[half, :, :], v[two]).then_inc(in3, 16)
            for n, name in enumerate(("s5_c_re_2", "s5_c_im_2")):
                sp.dma_start(craw[:, n, :, :], A[name][0].rearrange("g h p -> (g h) p").rearrange("(q r) p -> r q p", r=P)).then_inc(in3, 16)
            tiles.inc(2 + 3)
            tiles.inc(2 * S5T)
            for s in range(2):
                slot(8, glu_cols(A["w_s5_glu_2"][0], 512 * s, D + 512 * s, 512))
            for s in range(2):
                slot(4, thirds(A["w_out_2"][0], 8, 512 * s, 512))
            for e in done:
                sp.wait_ge(done[e], 29)
            sp.dma_start(memk, A["mem_2"][0].rearrange("(c p) d -> p c d", p=P)).then_inc(in3, 16)
            tiles.inc(NK)
            slot(4, thirds(A["w_xq_2"][0], 8, 0, 512))
            slot(4, thirds(A["w_xkv_2"][0], 8, 0, 512))
            slot(2, thirds(A["w_xkv_2"][0], 8, 512, 512))
            slot(8, quarter(A["w_xo_2"][0], 4, 0, 1024))
            slot(4, two_cols(A["w_sh_gu_2"][0], 0, 256, 256))
            slot(8, quarter(A["w_sh_down_2"][0], 2, 0, 1024))
            for e in done:
                sp.wait_ge(done[e], 36)
            sp.dma_start(wrt, A["w_router_2"][0].rearrange("(k p) n -> p k n", p=P)).then_inc(in3, 16)
            sp.dma_start(rbias, A["router_bias_2"][0].partition_broadcast(P)).then_inc(in3, 16)
            sp.dma_start(sc_c2, A["shape_constants"]).then_inc(in3, 16)
            def expert_weights(e, b, used=None):
                gu = A["w_exp_gu_2"][0].rearrange("e (k p) n -> p e k n", p=P)
                dn = A["w_exp_down_2"][0].rearrange("e (k p) n -> p e k n", p=P)
                pick = lambda ap: ap[:, e, :, :] if isinstance(e, int) else ap[:, bass.ds(e, 1), :, :].squeeze(1)
                gu, dn = pick(gu), pick(dn)
                dst = wgu[b][:, :].rearrange("p (k n) -> p k n", n=512)
                if used is not None:
                    sp.wait_ge(moe["gu"], used)
                for a, z in ((0, 3), (3, 6), (6, 8)):
                    sp.dma_start(dst[:, a:z, :], gu[:, a:z, :]).then_inc(wg_ready[b], 16)
                if used is not None:
                    sp.wait_ge(moe["down"], used)
                sp.dma_start(wdn[b], dn).then_inc(wd_ready[b], 16)

            tiles.inc(8)
            sp.wait_ge(tile_done, tiles.v)
            expert_weights(0, 0)
            expert_weights(1, 1)
            for e in done:
                sp.wait_ge(done[e], 37)
            expert_weights(2, 2)
            expert_weights(3, 3)
            with sp.Fori(0, NE // 4 - 1) as i:
                for k in range(4):
                    expert_weights(4 * i + 4 + k, k, 4 * i + 1 + k)
            for e in done:
                sp.wait_ge(done[e], 39)
            crowded = sp.value_load(cnti[0:1, 0:1])
            with sp.If(crowded > CAP):
                with sp.Fori(0, 3) as bb:
                    with sp.Fori(0, NE) as e:
                        expert_weights(e, 0, NE * bb + e + NE)
            with sp.Else():
                sp.nop()
            for e in done:
                sp.wait_ge(done[e], 40)
            sp.dma_start(g3, A["ln3_g_2"][0].partition_broadcast(P)).then_inc(fin_in, 16)
            sp.dma_start(b3, A["ln3_b_2"][0].partition_broadcast(P)).then_inc(fin_in, 16)
            for c in range(TC):
                sp.wait_ge(fin_in, 16 * (2 + c))
                sp.dma_start(fin[c], ytab[c * P:(c + 1) * P, :]).then_inc(fin_in, 16)
            for c in range(TC):
                sp.wait_ge(fin_ready, c + 1)
                sp.dma_start(out[0, c * P:(c + 1) * P, :], fin[c]).then_inc(out_sem, 16)
            sp.wait_ge(out_sem, 16 * TC)

        @block.gpsimd
        def _(pool):
            ph = Count()
            chain = Count()

            def link(ins):
                chain.inc()
                ins.then_inc(pool_chain, 1)
                pool.wait_ge(pool_chain, chain.v)

            def select(m, op, base, step, ch):
                link(nc.gpsimd.memset(m[:], 0.0 if op == ALU.not_equal else 1.0))
                link(nc.gpsimd.affine_select(out=m[:], in_=m[:], compare_op=op, fill=1.0 if op == ALU.not_equal else 0.0,
                                             base=base, pattern=[[step, P]], channel_multiplier=ch))

            nc.gpsimd.memset(ones[:], 1.0)
            select(ident, ALU.not_equal, 0, -1, 1)
            select(tri, ALU.is_ge, 0, 1, -1)
            select(stri, ALU.is_gt, 0, 1, -1)
            for k, v in enumerate((RMS_EPS, LN_EPS, 1.0, float(np.pi / 2))):
                nc.gpsimd.memset(kc[:, k:k + 1], v)
            for r in raw:
                nc.gpsimd.memset(r[:, 0:PAD], 0.0)
            pool.drain().then_inc(consts_ready, 1)
            for _ in range(23):
                phase_end(pool, "pool", ph)
            nc.gpsimd.iota(iot, pattern=[[1, T]], base=0, channel_multiplier=0, allow_small_or_imprecise_dtypes=True)
            for _ in range(24, 37):
                phase_end(pool, "pool", ph)
            G = nc.gpsimd
            G.iota(slotrow, pattern=[[1, P]], base=0, channel_multiplier=0, allow_small_or_imprecise_dtypes=True)
            link(G.iota(slotcol[:, 0:1], pattern=[[0, 1]], base=NTOK, channel_multiplier=1, allow_small_or_imprecise_dtypes=True))
            G.tensor_scalar(slotcol[:, 1:2], slotcol[:, 0:1], -1.0, None, ALU.mult)
            G.iota(rinfo[:, :, 0:1], pattern=[[P, TC], [0, NE]], base=0, channel_multiplier=1, allow_small_or_imprecise_dtypes=True)
            G.memset(rinfo[:, :, 1:2], 1.0)
            link(G.memset(zrow, 0.0))
            G.dma_start(xtab[NTOK:NTOK + P, :], zrow).then_inc(tok_out, 16)
            G.dma_start(ytab[NTOK:NTOK + P, :], zrow).then_inc(tok_out, 16)
            for n in range(2 * TC):
                before = TOK_TILES + 2 * n if n < TC else RES_TILES + 2 * (n - TC)
                pool.wait_ge(tile_evac, before + 2)
                pool.wait_ge(tok_out, 16 * (2 + n))
                tab = xtab if n < TC else ytab
                c = n % TC
                G.dma_start(tab[c * P:(c + 1) * P, :], tokb[n % 2]).then_inc(tok_out, 16)
            pool.wait_ge(tok_out, 16 * (2 + 2 * TC))
            phase_end(pool, "pool", ph)
            phase_end(pool, "pool", ph)

            def wait(s, x):
                if not (isinstance(x, int) and x <= 0):
                    pool.wait_ge(s, x)

            def m_gather(n, b, q):
                wait(moe["conv"], n + 1)
                wait(moe["turned"], n - 1)
                pool.nop().then_inc(wait_taken, 1)
                G.indirect_dma_start(out=xe[b], out_offset=None, in_=xtab,
                                     in_offset=bass.IndirectOffsetOnAxis(ap=sidx[q], axis=0)).then_inc(gathered[b], 16)

            def m_scatter(n, b, q):
                wait(moe["y0"], n + 1)
                wait(moe["y1"], n + 1)
                wait(moe["scattered"], 16 * n)
                pool.nop().then_inc(wait_taken, 1)
                G.indirect_dma_start(out=ytab, out_offset=bass.IndirectOffsetOnAxis(ap=sidx[q], axis=0), in_=ye[b],
                                     in_offset=None, compute_op=ALU.add).then_inc(moe["scattered"], 16)

            def m_step(e, k):
                if not isinstance(e, int) or e + 2 < NE:
                    m_gather(e + 2, k % 2, (k + 2) % 4)
                m_scatter(e, k % 2, k)

            m_gather(0, 0, 0)
            m_gather(1, 1, 1)
            for e in range(4):
                m_step(e, e)
            with pool.Fori(0, NE // 4 - 2) as i:
                for k in range(4):
                    m_step(4 * i + 4 + k, k)
            for e in range(NE - 4, NE):
                m_step(e, e % 4)
            pool.wait_ge(moe["scattered"], 16 * NE)
            phase_end(pool, "pool", ph)
            crowded = pool.value_load(cnti[0:1, 0:1])
            with pool.If(crowded > CAP):
                with pool.Fori(0, 3) as bb:
                    with pool.Fori(0, NE) as e:
                        n = NE * bb + e + NE
                        m_gather(n, 0, 0)
                        m_scatter(n, 0, 0)
                pool.wait_ge(moe["scattered"], 16 * 4 * NE)
            with pool.Else():
                pool.nop()
            phase_end(pool, "pool", ph)
            phase_end(pool, "pool", ph)

        @block.tensor
        def _(pe):
            ph = Count()
            tiles = Count()
            slots = Count()
            nsq, nstat = Count(), Count()
            nw, nx = Count(), Count()

            def slot_wait():
                r = slots.s % NSLOT
                pe.wait_ge(w_ready[r], 48 * (slots.s // NSLOT + 1) + 48 // NSLOT * slots.dyn)
                slots.inc()
                return wring[r]

            def y_square(y):
                pe.wait_ge(sq_ready, nsq.v + 1)
                nc.tensor.matmul(mp[0][:], ones[:], acc[y % NBANK][:], start=y == 0, stop=y == 15).then_inc(ysq_used, 1)
                nsq.inc()

            def tile(mms, lo=0, hi=P, n=T):
                b = tp[tiles.s % NBANK]
                if tiles.s >= NBANK:
                    pe.wait_ge(tile_evac, tiles.v - NBANK + 1)
                for k, (w, x) in enumerate(mms):
                    ins = nc.tensor.matmul(b[lo:hi, 0:n], w, x, start=k == 0, stop=k == len(mms) - 1)
                ins.then_inc(tile_done, 1)
                tiles.inc()

            def turn(srcs):
                b = tp[tiles.s % NBANK]
                if tiles.s >= NBANK:
                    pe.wait_ge(tile_evac, tiles.v - NBANK + 1)
                for k, src in enumerate(srcs):
                    m = src.shape[0]
                    n = src.shape[1]
                    ins = nc.tensor.transpose(b[0:n, k * P:k * P + m], src, ident[0:m, 0:m])
                ins.then_inc(tile_done, 1)
                tiles.inc()

            def proj(k, xs, n_tiles):
                w = slot_wait()
                w = w[:, 0:k * n_tiles * P].rearrange("p (k n) -> p k n", n=n_tiles * P)
                for m in range(n_tiles):
                    tile([(w[:, kk, m * P:(m + 1) * P], xs[:, kk, :]) for kk in range(k)])

            def proj_split(k, xhi, x, hi, order, fresh=False, each=None):
                r = slots.s % NSLOT
                slots.inc()
                n = len(order) * P
                parts = [b[:, 0:k * n].rearrange("p (k n) -> p k n", n=n) for b in (hi[r][1], wlo[r])]
                xparts = (xhi[1], x[1])
                for t, m in enumerate(order):
                    b = tp[tiles.s % NBANK]
                    pe.wait_ge(tile_evac, tiles.v - NBANK + 1)
                    for kk in range(k):
                        if t == 0 and kk in (0, -(-k // 2)):
                            pe.wait_ge(wlo_ready, nw.v + 1)
                            nw.inc()
                        if t == 0 and fresh:
                            pe.wait_ge(xlo_ready, nx.s + kk + 1)
                        for q, (wp, xp) in enumerate(((0, 0), (0, 1), (1, 0))):
                            ins = nc.tensor.matmul(b[:], parts[wp][:, kk, m * P:(m + 1) * P], xparts[xp][:, kk, :],
                                                   start=kk == 0 and q == 0, stop=kk == k - 1 and q == 2)
                    ins.then_inc(tile_done, 1)
                    tiles.inc()
                    if each is not None:
                        each(t)

            def proj_pairs(xs):
                w = slot_wait()[:, :].rearrange("p (k n) -> p k n", n=512)
                for m in (0, 2, 1, 3):
                    tile([(w[:, kk, m * P:(m + 1) * P], xs[:, kk, :]) for kk in range(NK)])

            def sum_squares(k, src, bank):
                for kk in range(k):
                    pe.wait_ge(sq_ready, nsq.v + 1)
                    ins = nc.tensor.matmul(mp[bank][:, 0:src.shape[2]], ones[:], src[:, kk, :], start=kk == 0, stop=kk == k - 1)
                    nsq.inc()
                ins.then_inc(stat_ready, 1)
                nstat.inc()

            def sum_plain(k, src, bank):
                for kk in range(k):
                    ins = nc.tensor.matmul(mp[bank][:, 0:src.shape[2]], ones[:], src[:, kk, :], start=kk == 0, stop=kk == k - 1)
                ins.then_inc(stat_ready, 1)
                nstat.inc()

            def layer_norm(k, src, centred_sq):
                sum_plain(k, src, 0)
                sum_squares(k, centred_sq, 1)

            def ssd_group(g, b, feed):
                act0, dve0 = (g + 1) * GPER["act"], (g + 1) * GPER["dve"]
                pe.wait_ge(core["dve"], dve0)
                pe.wait_ge(silu_ready, NBANK + 4 * g + 4)
                for ct in range(2):
                    for c in range(TC):
                        ins = nc.tensor.transpose(mp[ct][:, c * P:(c + 1) * P], xg[b][:, ct, c * P:(c + 1) * P], ident[:])
                    ins.then_inc(core["pe"], 1)
                for c in range(TC):
                    ins = nc.tensor.transpose(mp[2][:, c * P:(c + 1) * P], bg[b][:, c * P:(c + 1) * P], ident[:])
                ins.then_inc(core["pe"], 1)
                for c in range(TC):
                    s = slice(c * P, (c + 1) * P)
                    ins = nc.tensor.matmul(mp[3][:, s], bg[b][:, s], cg[b][:, s], start=True, stop=True)
                ins.then_inc(core["pe"], 1)
                for j in range(4):
                    pe.wait_ge(core["act"], act0 + (3, 4, 7, 10)[j])
                    if j >= 2:
                        pe.wait_ge(core["dve"], dve0 + 2 + j)
                    ins = nc.tensor.matmul(mp[j % 2][:], ones[0:HEADS, :], acsm[j % 2][0:HEADS, :], start=True, stop=True)
                    ins.then_inc(core["pe"], 1)
                pe.wait_ge(core["act"], act0 + 5)
                pe.wait_ge(core["dve"], dve0 + 3)
                for c in range(TC - 1):
                    bank = mp[2][:, c * 256:c * 256 + 256] if c < 2 else mp[3][:, 0:256]
                    ins = nc.tensor.matmul(bank, btk[:, c, :], xde[:, c, :], start=True, stop=True)
                    ins.then_inc(core["pe"], 1)
                feed()
                pe.wait_ge(core["dve"], dve0 + 18)
                for ct in range(2):
                    for c in range(TC):
                        s = slice(c * P, (c + 1) * P)
                        for jj in range(2):
                            j = 2 * ct + jj
                            o = mp[ct][64 * jj:64 * jj + 64, s]
                            ins = nc.tensor.matmul(o, xdt[:, c, 64 * j:64 * j + 64], sg[j][:, s], start=True, stop=c == 0)
                            if c:
                                ins = nc.tensor.matmul(o, st[c - 1][:, 64 * j:64 * j + 64], cts[:, j, s], start=False, stop=True)
                    ins.then_inc(core["pe"], 1)

            pe.wait_ge(consts_ready, 1)
            pe.wait_ge(param_in, 16 * len(par.rows))
            for b in range(0, NPB, 4):
                turn([pk[0:min(P, par.n - bb * P), bb, :] for bb in range(b, min(b + 4, NPB))])
            pe.wait_ge(x_in, 16)
            for k in range(NK):
                turn([xtok[:, c, k * P:(k + 1) * P] for c in range(TC)])
            phase_end(pe, "pe", ph)
            sum_squares(NK, sq, 0)
            phase_end(pe, "pe", ph)
            def project_group():
                w = slot_wait()[:, :].rearrange("p (k n) -> p k n", n=512)
                for m in range(4):
                    tile([(w[:, k, m * P:(m + 1) * P], uT[:, k, :]) for k in range(NK)])

            pe.wait_ge(misc_in, 16 * 5)
            for c in range(TC):
                for k in range(NK):
                    ins = nc.tensor.matmul(mp[0][:, c * HEADS:(c + 1) * HEADS], uT[:, k, c * P:(c + 1) * P], wdt[:, k, :],
                                           start=k == 0, stop=k == NK - 1)
            ins.then_inc(stat_ready, 1)
            nstat.inc()
            project_group()
            pe.wait_ge(dA_ready, 1)
            nc.tensor.matmul(mp[1][:, 0:P], tri[:], dA, start=True, stop=True)
            nc.tensor.matmul(mp[2][:, 0:P], ones[:], dA, start=True, stop=True)
            for c in range(TC):
                ins = nc.tensor.matmul(mp[3][0:HEADS, c * P:(c + 1) * P], dA[:, c * HEADS:(c + 1) * HEADS], tri[:],
                                       start=True, stop=True)
            ins.then_inc(stat_ready, 1)
            nstat.inc()
            phase_end(pe, "pe", ph)

            pe.nop().then_inc(core["pe"], GPER["pe"])
            with pe.Fori(0, 3) as i:
                tiles.enter(i, 8)
                slots.enter(i, 2)
                ssd_group(2 * i, 0, project_group)
                ssd_group(2 * i + 1, 1, project_group)
            tiles.leave(3)
            slots.leave(3)
            ssd_group(6, 0, project_group)
            ssd_group(7, 1, lambda: None)
            phase_end(pe, "pe", ph)
            for s in range(4):
                proj_split(NK, u_hi, u_lo, whi, range(4), fresh=s == 0, each=lambda m: y_square(4 * s + m - 2) if 4 * s + m >= 2 else None)
            nx.inc(NK)
            for y_tile in (14, 15):
                y_square(y_tile)
            phase_end(pe, "pe", ph)
            phase_end(pe, "pe", ph)
            for s in range(4):
                proj_split(16, yhi, y_lo, whi, range(2), fresh=s == 0)
            nx.inc(16)
            phase_end(pe, "pe", ph)

            def ffn():
                sum_squares(NK, sq, 0)
                phase_end(pe, "pe", ph)
                with pe.Fori(0, 5) as i:
                    tiles.enter(i, 8)
                    slots.enter(i, 2)
                    nw.enter(i, 4)
                    proj_split(NK, u_hi, u_lo, whi, (0, 2, 1, 3), fresh=True)
                    proj_split(NK, u_hi, u_lo, whi, (0, 2, 1, 3))
                tiles.leave(5)
                slots.leave(5)
                nw.leave(5)
                nx.inc(NK)
                proj_split(NK, u_hi, u_lo, whi, (0, 2, 1, 3))
                phase_end(pe, "pe", ph)
                with pe.Fori(0, 2) as i:
                    tiles.enter(i, 4)
                    slots.enter(i, 4)
                    nw.enter(i, 8)
                    for q in range(4):
                        proj_split(FFN_TILES, ffhi, ff_lo, wdhi, range(1), fresh=q == 0)
                tiles.leave(2)
                slots.leave(2)
                nw.leave(2)
                nx.inc(FFN_TILES)
                phase_end(pe, "pe", ph)

            ffn()
            sum_squares(NK, sq, 0)
            phase_end(pe, "pe", ph)
            for s in range(4):
                proj_pairs(uT)
            phase_end(pe, "pe", ph)
            layer_norm(NK, cv, lnsq)
            phase_end(pe, "pe", ph)
            for s in range(2):
                proj_split(NK, u_hi, u_lo, whi, range(4), fresh=s == 0)
            nx.inc(NK)
            phase_end(pe, "pe", ph)
            ffn()
            sum_squares(NK, sq, 0)
            phase_end(pe, "pe", ph)
            proj_split(NK, u_hi, h_lo, whi, range(4), fresh=True)
            nx.inc(NK)
            pe.wait_ge(in2, 16 * 5)
            for half in range(2):
                tile([(wkr[:, k, 32 * half:32 * half + 32], hT[:, k, :]) for k in range(NK)], lo=64, hi=96)
            for s in range(5):
                proj_split(NK, u_hi, h_lo, whi, range(4))
            phase_end(pe, "pe", ph)
            sum_squares(2, sq, 0)
            phase_end(pe, "pe", ph)
            sum_squares(2, sq, 0)
            phase_end(pe, "pe", ph)

            def head_proj(h):
                tile([(wuq[:, k, 96 * h:96 * h + 96], hq[:, k, :]) for k in range(2)], hi=96)
                tile([(wrot[:, k, h, :], hq[:, k, :]) for k in range(2)], lo=64, hi=96)
                tile([(wukv[:, k, P * h:P * h + 64], hkv[:, k, :]) for k in range(2)], hi=64)
                b = tp[tiles.s % NBANK]
                pe.wait_ge(tile_evac, tiles.v - NBANK + 1)
                for c in range(TC):
                    for k in range(2):
                        ins = nc.tensor.matmul(b[:, 64 * c:64 * c + 64], hkv[:, k, c * P:(c + 1) * P],
                                               wukv[:, k, P * h + 64:P * h + P], start=k == 0, stop=k == 1)
                ins.then_inc(tile_done, 1)
                tiles.inc()

            def attention(s, n_items, per_head, blocks, q, k, v, o, probs, turned, before):
                for n in range(n_items + 3):
                    if n < n_items:
                        before(n)
                        if n >= 2:
                            pe.wait_ge(s["masked"], n - 1)
                        nb = blocks(n)
                        nc.tensor.matmul(mp[n % 2][:, 0:nb * P], q(n), k(n, nb), start=True, stop=True).then_inc(s["scores"], 1)
                    m = n - 2
                    if 0 <= m < n_items:
                        pe.wait_ge(s["normed"], m + 1)
                        if m >= 1:
                            pe.wait_ge(s["evac"], m)
                        for j in range(blocks(m)):
                            ins = nc.tensor.transpose(mp[2][:, j * P:(j + 1) * P], probs[m % 3][:, j * P:(j + 1) * P], ident[:])
                        ins.then_inc(s["turned"], 1)
                    m = n - 3
                    if 0 <= m < n_items:
                        pe.wait_ge(s["evac"], m + 1)
                        if m % per_head == 0 and m:
                            pe.wait_ge(s["out"], m // per_head)
                        for j in range(blocks(m)):
                            ins = nc.tensor.matmul(o(m), v(m, j), turned[m % 2][:, j * P:(j + 1) * P],
                                                   start=j == 0, stop=j == blocks(m) - 1)
                        ins.then_inc(s["pv"], 1)

            def mla_before(n):
                h = n // TC
                if n == 0:
                    pe.wait_ge(heads_in, 16 * 6)
                    head_proj(0)
                if n % TC == 0:
                    pe.wait_ge(head_q, h + 1)
                if n % TC == 2 and h < 7:
                    head_proj(h + 1)

            attention(att[0], 32, 8, lambda n: n % TC + 1,
                      lambda n: qh[n // TC % 2][0:96, (n % TC) * P:(n % TC + 1) * P],
                      lambda n, nb: kh[n // TC % 2][0:96, 0:nb * P],
                      lambda n, j: vh[n // TC % 2][:, j, :],
                      lambda n: mp[3][64 * (n // TC % 2):64 * (n // TC % 2) + 64, (n % TC) * P:(n % TC + 1) * P],
                      pb, pt, mla_before)
            phase_end(pe, "pe", ph)
            proj(4, attnT, 8)
            phase_end(pe, "pe", ph)
            phase_end(pe, "pe", ph)
            for b in (bda, bdb):
                turn([b[:, 4 * q:4 * q + 4, :].rearrange("p a b -> p (a b)") for q in range(4)])
            for n in (0, 0, 1):
                turn([cbig[:, n, q, :] for q in range(4)])
            phase_end(pe, "pe", ph)
            for j in range(S5T + 1):
                if j < S5T:
                    q, r = j // 4, slice(32 * (j % 4), 32 * (j % 4) + 32)
                    for b in (btr, bti):
                        tile([(b[r, q, :], us[r, q, :])])
                if j >= 1:
                    m = j - 1
                    q, r = m // 4, slice(32 * (m % 4), 32 * (m % 4) + 32)
                    for n, c in enumerate((ctr, ctn, cti, cti)):
                        pe.wait_ge(s5_c, 4 * m + n + 1)
                        ins = nc.tensor.matmul(mp[q][r, :], c[:, q, r], pr5[n][:], start=n == 0, stop=n == 3)
                        ins.then_inc(s5_yd, 1)
            phase_end(pe, "pe", ph)
            phase_end(pe, "pe", ph)
            for s in range(2):
                proj_split(4, us_hi, us_lo, wdhi, (4, 0, 5, 1, 6, 2, 7, 3), fresh=s == 0)
            nx.inc(4)
            phase_end(pe, "pe", ph)
            for s in range(2):
                proj_split(NK, gm_hi, gm_lo, wdhi, range(4), fresh=s == 0)
            nx.inc(NK)
            phase_end(pe, "pe", ph)
            layer_norm(NK, hT, gs)
            phase_end(pe, "pe", ph)
            pe.wait_ge(in3, 16 * 9)
            for k in range(NK):
                turn([memk[:, c, k * P:(k + 1) * P] for c in range(2)])
            phase_end(pe, "pe", ph)
            layer_norm(NK, memT, memq)
            phase_end(pe, "pe", ph)
            proj(NK, hT, 4)
            w = slot_wait()[:, :].rearrange("p (k n) -> p k n", n=512)
            for m in range(4):
                tile([(w[:, k, m * P:(m + 1) * P], mT[:, k, :]) for k in range(NK)], n=256)
            w = slot_wait()[:, :].rearrange("p (k n) -> p k n", n=512)
            for c in range(2):
                tile([(mT[:, k, c * P:(c + 1) * P], w[:, k, :]) for k in range(NK)])
            phase_end(pe, "pe", ph)
            attention(att[1], 16, 4, lambda n: 2,
                      lambda n: qx[:, n // TC, (n % TC) * P:(n % TC + 1) * P],
                      lambda n, nb: kx[:, n // TC, :],
                      lambda n, j: vx[:, j, (n // TC) * P:(n // TC + 1) * P],
                      lambda n: mp[3][:, (n % TC) * P:(n % TC + 1) * P],
                      xpb, xpt, lambda n: None)
            phase_end(pe, "pe", ph)
            proj(4, ox, 8)
            phase_end(pe, "pe", ph)
            layer_norm(NK, hT, uT)
            phase_end(pe, "pe", ph)
            pe.wait_ge(in3, 16 * 12)
            for c in range(TC):
                for k in range(NK):
                    ins = nc.tensor.matmul(mp[0][:, c * NE:(c + 1) * NE], hT[:, k, c * P:(c + 1) * P], wrt[:, k, :],
                                           start=k == 0, stop=k == NK - 1)
            ins.then_inc(rt["logits"], 1)
            for c in range(TC):
                for half in range(2):
                    turn([hT[:, 4 * half + k, c * P:(c + 1) * P] for k in range(4)])
            proj_pairs(hT)
            pe.wait_ge(glu_ready, 2 + 2 * FFN_TILES + 8 + 8 + 2)
            proj(2, sact, 8)
            assert tiles.s == RES_TILES
            pe.wait_ge(conv_ready, NBANK + CONVS)
            for c in range(TC):
                for half in range(2):
                    turn([sq[:, 4 * half + k, c * P:(c + 1) * P] for k in range(4)])
            phase_end(pe, "pe", ph)
            for c in range(TC):
                for c1 in range(c):
                    nc.tensor.matmul(mp[1][:, c * NE:(c + 1) * NE], ones[:], mask[:, c1 * NE:(c1 + 1) * NE], start=c1 == 0, stop=False)
                nc.tensor.matmul(mp[1][:, c * NE:(c + 1) * NE], stri[:], mask[:, c * NE:(c + 1) * NE], start=c == 0, stop=True)
            for c in range(TC):
                ins = nc.tensor.matmul(mp[2][:, 0:NE], ones[:], mask[:, c * NE:(c + 1) * NE], start=c == 0, stop=c == TC - 1)
            ins.then_inc(rt["pos"], 1)
            phase_end(pe, "pe", ph)

            def pos(x):
                return None if isinstance(x, int) and x <= 0 else x

            def wait(s, x):
                if pos(x) is not None:
                    pe.wait_ge(s, x)

            def m_idx(e, n, b):
                wait(moe["onehot"], n + 1)
                wait(moe["conv"], n)
                for c in range(TC):
                    ins = nc.tensor.matmul(mp[1][:, 0:3], oneh[b][:, c, :], at(rinfo, c * NE + e), start=c == 0, stop=c == TC - 1)
                ins.then_inc(moe["idx"], 1)

            def m_turn(n, b, g_value):
                pe.wait_ge(gathered[b], g_value)
                wait(moe["xT"], n)
                for k in range(NK):
                    ins = nc.tensor.transpose(tp[2 + k // 4][:, (k % 4) * P:(k % 4 + 1) * P], xe[b][:, k * P:(k + 1) * P], ident[:])
                ins.then_inc(moe["turned"], 1)

            def m_gu(n, b, q, w_value):
                pe.wait_ge(wg_ready[q], w_value)
                wait(moe["xT"], n + 1)
                wait(moe["act"], n - 1)
                w = wgu[q][:, :].rearrange("p (k n) -> p k n", n=512)
                for k in range(NK):
                    ins = nc.tensor.matmul(tp[b][:], xeT[b][:, k, :], w[:, k, :], start=k == 0, stop=k == NK - 1)
                ins.then_inc(moe["gu"], 1)

            def m_actturn(n):
                wait(moe["act"], n + 1)
                wait(moe["actT"], n)
                for k in range(2):
                    ins = nc.tensor.transpose(mp[0][:, k * P:(k + 1) * P], actE[:, k * P:(k + 1) * P], ident[:])
                ins.then_inc(moe["actturned"], 1)

            def m_down(n, q, w_value):
                wait(moe["actT"], n + 1)
                pe.wait_ge(wd_ready[q], w_value)
                wait(moe["y0"], n)
                wait(moe["y1"], n)
                for half in range(2):
                    for k in range(2):
                        ins = nc.tensor.matmul(mp[2 + half][:], actET[:, k, :], wdn[q][:, k, 512 * half:512 * half + 512],
                                               start=k == 0, stop=k == 1)
                ins.then_inc(moe["down"], 1)

            def m_step(e, k):
                b = k % 2
                half = (e - b) // 2 if isinstance(e, int) else None
                turn_no = half if half is not None else (loop_i * 2 + 2 + k // 2)
                loads = (e - k) // 4 + 1 if isinstance(e, int) else loop_i + 2
                m_gu(e, b, k, 48 * loads)
                if not isinstance(e, int) or e + 1 < NE:
                    m_turn(e + 1, 1 - b, 16 * (turn_no + 1 + b))
                m_actturn(e)
                if not isinstance(e, int) or e + 2 < NE:
                    m_idx(e + 2, e + 2, b)
                m_down(e, k, 16 * loads)

            m_idx(0, 0, 0)
            m_idx(1, 1, 1)
            m_turn(0, 0, 16)
            for e in range(4):
                m_step(e, e)
            with pe.Fori(0, NE // 4 - 2) as loop_i:
                for k in range(4):
                    m_step(4 * loop_i + 4 + k, k)
            for e in range(NE - 4, NE):
                m_step(e, e % 4)
            phase_end(pe, "pe", ph)
            crowded = pe.value_load(cnti[0:1, 0:1])
            with pe.If(crowded > CAP):
                with pe.Fori(0, 3) as bb:
                    with pe.Fori(0, NE) as e:
                        n = NE * bb + e + NE
                        m_idx(e, n, 0)
                        m_turn(n, 0, NE * 16 * bb + 16 * e + 16 * (NE // 2 + 1))
                        m_gu(n, 0, 0, NE * 48 * bb + 48 * e + 48 * (NE // 4 + 1))
                        m_actturn(n)
                        m_down(n, 0, NE * 16 * bb + 16 * e + 16 * (NE // 4 + 1))
            with pe.Else():
                pe.nop()
            phase_end(pe, "pe", ph)
            phase_end(pe, "pe", ph)

        @block.scalar
        def _(act):
            ph = Count()
            tiles = Count()
            nsq, nstat, nstd = Count(), Count(), Count()
            nconv, nsilu, nxc, nln, nglu = Count(), Count(), Count(), Count(), Count()
            chain = Count()

            def link(ins):
                chain.inc()
                ins.then_inc(act_chain, 1)
                act.wait_ge(act_chain, chain.v)

            def take(dst, func=ACT.Copy, bias=None, lo=0, hi=P, n=T, scale=1.0):
                act.wait_ge(tile_done, tiles.v + 1)
                b = tp[tiles.s % NBANK]
                kw = {} if bias is None else {"bias": bias}
                nc.scalar.activation(dst, b[lo:hi, 0:n], func, scale=scale, **kw).then_inc(tile_evac, 1)
                tiles.inc()

            def take_raw(func=ACT.Copy, bias=None):
                act.wait_ge(conv_ready, nconv.v + 1)
                kw = {} if bias is None else {"bias": bias}
                take(raw[tiles.s % NBANK][:, PAD:PAD + T], func, **kw)
                nconv.inc()

            slots = Count(8)

            def split_half(r, hi, a, b):
                nc.scalar.activation(hi[r][1][:, a:b], wring[r][:, a:b], ACT.Copy).then_inc(whi_ready, 1)

            def slot_in():
                r = slots.s % NSLOT
                act.wait_ge(w_ready[r], 48 * (slots.s // NSLOT + 1) + 48 // NSLOT * slots.dyn)
                slots.inc()
                return r

            def split_weight(hi, k, n):
                r = slot_in()
                for a, b in halves(k, n):
                    split_half(r, hi, a, b)

            def split_x(x, hi, ks):
                for kk in ks:
                    nc.scalar.activation(hi[1][:, kk, :], x[0][:, kk, :], ACT.Copy).then_inc(xhi_ready, 1)

            def split_both(hi, k, n, x, xhi):
                r = slot_in()
                half = -(-k // 2)
                for (a, b), ks in zip(halves(k, n), (range(half), range(half, k))):
                    split_half(r, hi, a, b)
                    split_x(x, xhi, ks)

            def squares(k, src, dst):
                for kk in range(k):
                    nc.scalar.activation(dst[:, kk, :], src[:, kk, :], ACT.Square).then_inc(sq_ready, 1)
                    nsq.inc()

            def root(bank, width, eps, n=T):
                act.wait_ge(stat_ready, nstat.v + 1)
                nc.scalar.activation(std[:, 0:n], mp[bank][:, 0:n], ACT.Sqrt, scale=1.0 / width, bias=kc[:, eps:eps + 1])\
                  .then_inc(std_ready, 1)
                nstat.inc()

            def layer_norm(k, centred, centred_sq, out_, func, bias, n=T):
                nstat.inc()
                for kk in range(k):
                    act.wait_ge(xc_ready, nxc.v + 1)
                    nc.scalar.activation(centred_sq[:, kk, :], centred[:, kk, :], ACT.Square).then_inc(sq_ready, 1)
                    nxc.inc()
                    nsq.inc()
                root(1, k * P, 1, n)
                for kk in range(k):
                    act.wait_ge(ln_ready, nln.v + 1)
                    nc.scalar.activation(out_[:, kk, :], centred[:, kk, :], func, bias=bias(kk))
                    nln.inc()

            def ssd_rows(g, js):
                for j in js:
                    nc.scalar.activation(acsm[j % 2][0:HEADS, :], acsT[0:HEADS, :], ACT.Copy,
                                         scale=col(ident[0:HEADS, :], 4 * g + j)).then_inc(core["act"], 1)

            def ssd_group(g, b, feed):
                pe0, dve0 = (g + 1) * GPER["pe"], (g + 1) * GPER["dve"]
                act.wait_ge(core["pe"], pe0)
                ssd_rows(g, (0, 1))
                for ct in range(2):
                    act.wait_ge(core["pe"], pe0 + 1 + ct)
                    dst = xtk[:, :, ct * P:(ct + 1) * P]
                    src = mp[ct][:].rearrange("p (c n) -> p c n", n=P)
                    nc.scalar.activation(dst, src, ACT.Copy).then_inc(core["act"], 1)
                act.wait_ge(core["pe"], pe0 + 3)
                nc.scalar.activation(btk, mp[2][:].rearrange("p (c n) -> p c n", n=P), ACT.Copy).then_inc(core["act"], 1)
                for j in range(4):
                    act.wait_ge(core["pe"], pe0 + 5 + j)
                    nc.scalar.activation(ea[j][:], mp[j % 2][:], ACT.Exp).then_inc(core["act"], 1)
                    if j < 2:
                        ssd_rows(g, (j + 2,))
                    act.wait_ge(core["dve"], dve0 + 4 + j)
                    nc.scalar.activation(sg[j][:], sg[j][:], ACT.Exp).then_inc(core["act"], 1)
                feed()

            act.wait_ge(consts_ready, 1)
            for b in range(0, NPB, 4):
                n = min(4 * P, par.n - b * P)
                take(pcol[:, b * P:b * P + n], n=n)
            for k in range(NK):
                take(hT[:, k, :])
            phase_end(act, "act", ph)
            squares(NK, hT, sq)
            root(0, D, 0)
            phase_end(act, "act", ph)
            nstat.inc(2)
            act.wait_ge(misc_in, 16 * 5)
            act.wait_ge(negabs_ready, 1)
            link(nc.scalar.activation(dtk, dA, ACT.Exp))
            link(nc.scalar.activation(dtk, dtk, ACT.Ln, bias=kc[:, 2:3]))
            nc.scalar.activation(alog, alog, ACT.Exp).then_inc(softplus_ready, 1)
            act.wait_ge(dend_ready, 1)
            nc.scalar.activation(dend, dend, ACT.Exp).then_inc(softplus_ready, 1)
            phase_end(act, "act", ph)

            def take_group(g, b, first=False):
                if not first:
                    act.wait_ge(core["dve"], g * GPER["dve"])
                dst = [xg[b][:, 0, :], xg[b][:, 1, :], bg[b][:], cg[b][:]]
                for q in range(5):
                    if q < 4:
                        take_raw()
                    if q >= 1:
                        act.wait_ge(conv_ready, NBANK + nsilu.v + 1)
                        nc.scalar.activation(dst[q - 1], acc[q - 1][:], ACT.Silu).then_inc(silu_ready, 1)
                        nsilu.inc()

            act.nop().then_inc(core["act"], GPER["act"])
            act.nop().then_inc(silu_ready, NBANK)
            take_group(0, 0, first=True)
            with act.Fori(0, 3) as i:
                for c in (tiles, nconv, nsilu):
                    c.enter(i, 8)
                ssd_group(2 * i, 0, lambda: take_group(2 * i + 1, 1))
                ssd_group(2 * i + 1, 1, lambda: take_group(2 * i + 2, 0))
            for c in (tiles, nconv, nsilu):
                c.leave(3)
            ssd_group(6, 0, lambda: take_group(7, 1))
            ssd_group(7, 1, lambda: None)
            phase_end(act, "act", ph)
            split_both(whi, NK, 512, u_lo, u_hi)
            for m in range(16 + 1):
                if m < 16:
                    take_raw(ACT.Silu)
                if m % 4 == 2:
                    split_weight(whi, *((NK, 512) if m < 12 else (16, 256)))
                if m >= 1:
                    y = m - 1
                    act.wait_ge(conv_ready, nconv.v - (1 if m < 16 else 0) + NBANK)
                    if y >= NBANK:
                        act.wait_ge(ysq_used, y - NBANK + 1)
                    nc.scalar.activation(acc[y % NBANK][:], yT[:, y, :], ACT.Square).then_inc(sq_ready, 1)
                    nsq.inc()
            phase_end(act, "act", ph)
            nc.scalar.activation(std[:], mp[0][:], ACT.Sqrt, scale=1.0 / D_INNER, bias=kc[:, 0:1]).then_inc(std_ready, 1)
            phase_end(act, "act", ph)
            split_x(y_lo, yhi, range(16))
            for m in range(NK):
                take_raw()
                if m % 2 == 0:
                    split_weight(whi, *((16, 256) if m < 6 else (NK, 512)))
            phase_end(act, "act", ph)

            def ffn():
                squares(NK, hT, sq)
                root(0, D, 0)
                phase_end(act, "act", ph)

                def pair(p):
                    take_raw()
                    take_raw()
                    act.wait_ge(conv_ready, NBANK - 1 + nconv.v)
                    act.wait_ge(glu_ready, nglu.v + 1)
                    nc.scalar.activation(sgate[p % 2][:], acc[(2 * p) % NBANK][:], ACT.Silu).then_inc(silu_ready, 1)
                    nglu.inc()
                    nsilu.inc()

                split_x(u_lo, u_hi, range(NK))
                with act.Fori(0, 5) as i:
                    tiles.enter(i, 8), nconv.enter(i, 8), nsilu.enter(i, 4), nglu.enter(i, 4), slots.enter(i, 2)
                    for p in range(4):
                        pair(p)
                        if p % 2 == 0:
                            split_weight(whi, NK, 512)
                tiles.leave(5), nconv.leave(5), nsilu.leave(5), nglu.leave(5), slots.leave(5)
                for p in range(2):
                    pair(p)
                phase_end(act, "act", ph)
                split_both(wdhi, FFN_TILES, P, ff_lo, ffhi)
                for m in range(NK):
                    if m + 1 < NK:
                        split_weight(wdhi, FFN_TILES, P)
                    take_raw()
                phase_end(act, "act", ph)

            ffn()
            squares(NK, hT, sq)
            root(0, D, 0)
            phase_end(act, "act", ph)
            for j in range(NK):
                act.wait_ge(glu_ready, nglu.v + 1)
                take(glu_a[j % 2][:], ACT.Identity, bias=pc("pw1_b", j))
                take(glu_b[j % 2][:], ACT.Sigmoid, bias=pc("pw1_b", NK + j))
                nglu.inc()
            phase_end(act, "act", ph)
            slots.inc(4)
            split_weight(whi, NK, 512)
            layer_norm(NK, xc, lnsq, uT, ACT.Silu, lambda kk: pc("ln_b", kk))
            phase_end(act, "act", ph)
            split_x(u_lo, u_hi, range(NK))
            for m in range(NK):
                take_raw(ACT.Identity, bias=pc("pw2_b", m))
                if m % 4 == 1:
                    split_weight(whi, NK, 512)
            phase_end(act, "act", ph)
            ffn()
            squares(NK, hT, sq)
            root(0, D, 0)
            phase_end(act, "act", ph)
            split_both(whi, NK, 512, h_lo, u_hi)
            for n, dst in enumerate((hq[:, 0, :], hq[:, 1, :], hkv[:, 0, :], hkv[:, 1, :])):
                take(dst)
                if n == 1:
                    split_weight(whi, NK, 512)
            take(kro[64:96, :], lo=64, hi=96)
            take(krr[64:96, :], lo=64, hi=96)
            for n in range(4 + 2 * NK):
                if n < 4:
                    take(us[:, n, :])
                else:
                    take((gm if n < 4 + NK else gs)[:, (n - 4) % NK, :], ACT.Sigmoid)
                if n % 4 == 1 and n < 16:
                    split_weight(whi, NK, 512)
            phase_end(act, "act", ph)
            squares(2, hq, sq)
            root(0, 256, 0)
            for n, dst in enumerate((sinT, cosT)):
                act.wait_ge(ang_ready, n + 1)
                nc.scalar.activation(dst[64:96, :], dst[64:96, :], ACT.Sin).then_inc(sin_ready, 1)
            phase_end(act, "act", ph)
            squares(2, hkv, sq)
            root(0, 256, 0)
            phase_end(act, "act", ph)

            def head_take(h):
                b = h % 2
                if h >= 2:
                    act.wait_ge(att[0]["pv"], 4 * (h - 1))
                take(qh[b][0:96, :], hi=96)
                if h >= 1:
                    act.wait_ge(head_q, h)
                take(rq[64:96, :], lo=64, hi=96)
                take(kh[b][0:64, :], hi=64)
                take(vh[b].rearrange("p a b -> p (a b)"), n=256)
                nc.scalar.activation(kh[b][64:96, :], kro[64:96, :], ACT.Copy).then_inc(sin_ready, 1)

            def attention(s, n_items, blocks, scale, probs, turned, nmx, rsm, after):
                for n in range(n_items + 2):
                    if n < n_items:
                        act.wait_ge(s["masked"], n + 1)
                        p = probs[n % 3][:, 0:blocks(n) * P]
                        nc.scalar.activation(p, p, ACT.Exp, scale=scale, bias=nmx[:, n:n + 1],
                                             accum_out=rsm[:, n:n + 1]).then_inc(s["exped"], 1)
                        after(n)
                    m = n - 2
                    if m >= 0:
                        act.wait_ge(s["turned"], m + 1)
                        if m >= 2:
                            act.wait_ge(s["pv"], m - 1)
                        nc.scalar.activation(turned[m % 2][:, 0:blocks(m) * P], mp[2][:, 0:blocks(m) * P], ACT.Copy)\
                          .then_inc(s["evac"], 1)

            head_take(0)
            attention(att[0], 32, lambda n: n % TC + 1, MLA_SCALE, pb, pt, nmax, rsum,
                      lambda n: head_take(n // TC + 1) if n % TC == 2 and n // TC < 7 else None)
            phase_end(act, "act", ph)
            for m in range(NK):
                take_raw()
            phase_end(act, "act", ph)
            S = lambda k: s5p[:, k, :]
            act.wait_ge(in3, 16 * 8)
            link(nc.scalar.activation(S(0), ldt, ACT.Exp))
            act.nop().then_inc(s5_a, 1)
            act.wait_ge(s5_cat, 1)
            nc.scalar.activation(S(1), S(1), ACT.Exp).then_inc(s5_a, 1)
            act.wait_ge(s5_cat, 2)
            nc.scalar.activation(S(3), S(3), ACT.Sin)
            nc.scalar.activation(S(4), S(4), ACT.Sin).then_inc(s5_a, 1)
            phase_end(act, "act", ph)
            take(btr.rearrange("p a b -> p (a b)"))
            take(bti.rearrange("p a b -> p (a b)"))
            take(ctr.rearrange("p a b -> p (a b)"))
            take(ctn.rearrange("p a b -> p (a b)"), scale=-1.0)
            take(cti.rearrange("p a b -> p (a b)"), scale=-1.0)
            phase_end(act, "act", ph)
            for j in range(S5T):
                act.wait_ge(s5_ph, 2 * j + 1)
                nc.scalar.activation(st5[j % 2], st5[j % 2], ACT.Sin, scale=TWO_PI_DOWN).then_inc(sin_ready, 1)
                act.wait_ge(s5_ph, 2 * j + 2)
                nc.scalar.activation(ct5[j % 2], ct5[j % 2], ACT.Sin, scale=TWO_PI_DOWN).then_inc(sin_ready, 1)
                if j >= 1:
                    act.wait_ge(s5_b, j)
                take(acc[0][:])
                take(acc[1][:])
            phase_end(act, "act", ph)
            for q in range(4):
                act.wait_ge(s5_cat, 3 + q)
                nc.scalar.activation(us[:, q, :], us[:, q, :], ACT.Gelu_apprx_tanh)
            phase_end(act, "act", ph)
            slots.inc()
            split_both(wdhi, 4, 1024, us_lo, us_hi)
            for m in range(NK):
                act.wait_ge(glu_ready, nglu.v + 1)
                take(zr[m % 2], ACT.Sigmoid)
                take_raw()
                nglu.inc()
                if m % 4 == 1:
                    split_weight(wdhi, *((4, 1024) if m < 4 else (NK, 512)))
            phase_end(act, "act", ph)
            split_x(gm_lo, gm_hi, range(NK))
            for m in range(NK):
                take_raw()
                if m == 1:
                    split_weight(wdhi, NK, 512)
            phase_end(act, "act", ph)
            layer_norm(NK, xc, gs, hT, ACT.Identity, lambda kk: pc("ln1_b", kk))
            phase_end(act, "act", ph)
            for k in range(NK):
                take(memT[:, k, :], n=256)
            phase_end(act, "act", ph)
            layer_norm(NK, memc, memq, mT, ACT.Identity, lambda kk: pc("mem_ln_b", kk), n=256)
            phase_end(act, "act", ph)
            for m in range(4):
                take(qx[:, m, :])
            for m in range(4):
                take(kx[:, m, :], n=256)
            for m in range(2):
                take(vx[:, m, :])
            phase_end(act, "act", ph)
            attention(att[1], 16, lambda n: 2, X_SCALE, xpb, xpt, xsm[1], xsm[2], lambda n: None)
            phase_end(act, "act", ph)
            for m in range(NK):
                take_raw()
            phase_end(act, "act", ph)
            layer_norm(NK, xc, uT, hT, ACT.Identity, lambda kk: pc("ln2_b", kk))
            phase_end(act, "act", ph)
            act.wait_ge(rt["logits"], 1)
            nc.scalar.activation(scr, mp[0][:, 0:TC * NE], ACT.Sigmoid).then_inc(rt["scores"], 1)

            def take_rows(ns):
                for n in ns:
                    for half in range(2):
                        if n >= 2 and half == 0:
                            act.wait_ge(tok_out, 16 * (n - 1 + 2))
                        take(tokb[n % 2][:, 512 * half:512 * half + 512])

            take_rows(range(TC))
            for j in range(2):
                act.wait_ge(glu_ready, nglu.v + 1)
                take(ssil[j], ACT.Silu)
                take_raw()
                nglu.inc()
            for m in range(NK):
                take_raw()
            take_rows(range(TC, 2 * TC))
            phase_end(act, "act", ph)
            phase_end(act, "act", ph)

            def wait(s, x):
                if not (isinstance(x, int) and x <= 0):
                    act.wait_ge(s, x)

            def m_silu(n, b):
                wait(moe["gu"], n + 1)
                wait(moe["act"], n)
                nc.scalar.activation(silg, tp[b][:, 0:256], ACT.Silu).then_inc(moe["silu"], 1)

            def m_xT(n, b):
                wait(moe["turned"], n + 1)
                wait(moe["gu"], n - 1)
                for half in range(2):
                    ins = nc.scalar.activation(xeT[b][:, 4 * half:4 * half + 4, :],
                                               tp[2 + half][:].rearrange("p (k n) -> p k n", n=P), ACT.Copy)
                ins.then_inc(moe["xT"], 1)

            def m_actT(n):
                wait(moe["actturned"], n + 1)
                wait(moe["down"], n)
                nc.scalar.activation(actET, mp[0][:, 0:256].rearrange("p (k n) -> p k n", n=P), ACT.Copy).then_inc(moe["actT"], 1)

            def m_y0(n, b):
                wait(moe["down"], n + 1)
                wait(moe["scattered"], 16 * n - 16)
                nc.scalar.activation(ye[b][:, 0:512], mp[2][:], ACT.Copy).then_inc(moe["y0"], 1)

            def m_step(e, k):
                b = k % 2
                m_silu(e, b)
                if not isinstance(e, int) or e + 1 < NE:
                    m_xT(e + 1, 1 - b)
                m_actT(e)
                m_y0(e, b)

            m_xT(0, 0)
            for e in range(4):
                m_step(e, e)
            with act.Fori(0, NE // 4 - 2) as i:
                for k in range(4):
                    m_step(4 * i + 4 + k, k)
            for e in range(NE - 4, NE):
                m_step(e, e % 4)
            phase_end(act, "act", ph)
            crowded = act.value_load(cnti[0:1, 0:1])
            with act.If(crowded > CAP):
                with act.Fori(0, 3) as bb:
                    with act.Fori(0, NE) as e:
                        n = NE * bb + e + NE
                        m_xT(n, 0)
                        m_silu(n, 0)
                        m_actT(n)
                        m_y0(n, 0)
            with act.Else():
                act.nop()
            phase_end(act, "act", ph)
            for c in range(TC):
                act.wait_ge(var_ready, c + 1)
                nc.scalar.activation(rs3[:, c:c + 1], mv[:, c, 1:2], ACT.Sqrt, bias=kc[:, 1:2]).then_inc(rs_ready, 1)
            phase_end(act, "act", ph)

        @block.vector
        def _(dve):
            ph = Count()
            chain = Count()
            tiles = Count()
            nconv, nsilu, nstat, nstd, nglu = Count(), Count(), Count(), Count(), Count()
            V = nc.vector

            def link(ins):
                chain.inc()
                ins.then_inc(dve_chain, 1)
                dve.wait_ge(dve_chain, chain.v)

            slots = Count(8)
            nw, nx = Count(), Count()

            def split_half(r, hi, a, b):
                dve.wait_ge(whi_ready, nw.v + 1)
                V.tensor_tensor(wlo[r][:, a:b], wring[r][:, a:b], hi[r][1][:, a:b].bitcast(F32), ALU.subtract).then_inc(wlo_ready, 1)
                nw.inc()

            def split_weight(hi, k, n):
                r = slots.s % NSLOT
                slots.inc()
                for a, b in halves(k, n):
                    split_half(r, hi, a, b)

            def split_x(x, hi, ks):
                for kk in ks:
                    dve.wait_ge(xhi_ready, nx.v + 1)
                    V.tensor_tensor(x[1][:, kk, :], x[0][:, kk, :], hi[1][:, kk, :].bitcast(F32), ALU.subtract).then_inc(xlo_ready, 1)
                    nx.inc()

            def split_both(hi, k, n, x, xhi):
                r = slots.s % NSLOT
                slots.inc()
                half = -(-k // 2)
                for (a, b), ks in zip(halves(k, n), (range(half), range(half, k))):
                    split_half(r, hi, a, b)
                    split_x(x, xhi, ks)

            def norm_scale(k, src, dst, gain, last=None, n=T):
                dve.wait_ge(std_ready, nstd.v + 1)
                nstd.inc()
                link(V.reciprocal(rinv[:, 0:n], std[:, 0:n]))
                for kk in range(k):
                    ins = V.scalar_tensor_tensor(dst[:, kk, :], src[:, kk, :], gain(kk), rinv[:, 0:n], ALU.mult, ALU.mult)
                    if last is not None:
                        ins.then_inc(last, 1)

            def layer_norm(k, src, centred, gain, n=T):
                dve.wait_ge(stat_ready, nstat.v + 1)
                nstat.inc()
                link(V.tensor_scalar(rinv[:, 0:n], mp[0][:, 0:n], 1.0 / (k * P), None, ALU.mult))
                for kk in range(k):
                    V.tensor_tensor(centred[:, kk, :], src[:, kk, :], rinv[:, 0:n], ALU.subtract).then_inc(xc_ready, 1)
                nstat.inc()
                norm_scale(k, centred, centred, gain, last=ln_ready, n=n)

            def convolve(taps, w, bias, dst):
                r = raw[tiles.s % NBANK]
                dve.wait_ge(tile_evac, tiles.v + 1)
                link(V.tensor_scalar(dst, r[:, PAD:PAD + T], w(taps - 1), bias, ALU.mult, ALU.add))
                for t in range(1, taps):
                    ins = V.scalar_tensor_tensor(dst, r[:, PAD - t:PAD - t + T], w(taps - 1 - t), dst, ALU.mult, ALU.add)
                    if t < taps - 1:
                        link(ins)
                tiles.inc()
                nconv.inc()
                ins.then_inc(conv_ready, 1)

            def residual(m, scale=None):
                r = raw[tiles.s % NBANK][:, PAD:PAD + T]
                dve.wait_ge(tile_evac, tiles.v + 1)
                h = at(hT, m)
                if scale is None:
                    ins = V.tensor_tensor(h, h, r, ALU.add)
                else:
                    ins = V.scalar_tensor_tensor(h, h, scale, r, ALU.mult, ALU.add)
                tiles.inc()
                nconv.inc()
                ins.then_inc(conv_ready, 1)

            def conv_group(g):
                for q in range(4):
                    c = 2 * g + q if q < 2 else (16 + g if q == 2 else 24 + g)
                    dve.wait_ge(silu_ready, nsilu.v + 1)
                    convolve(4, lambda t: pc("a_conv_w", 32 * t + c), pc("a_conv_b", c), acc[q][:])
                    nsilu.inc()

            def ssd_group(g, b, feed):
                pe0, act0 = (g + 1) * GPER["pe"], (g + 1) * GPER["act"]
                dve.wait_ge(core["pe"], pe0 + 4)
                m3 = mp[3][:].rearrange("p (c n) -> p c n", n=P)
                V.tensor_tensor(cbm, m3, tri[:].unsqueeze(1).broadcast_to([P, TC, P]), ALU.mult).then_inc(core["dve"], 1)
                dve.wait_ge(core["act"], act0 + 4)
                four = lambda ap: cols_of(ap, 4 * g)
                for c in range(TC):
                    x4 = xtk[:, c, :].rearrange("p (h n) -> p h n", n=64)
                    ins = V.tensor_tensor(xdt[:, c, :].rearrange("p (h n) -> p h n", n=64), x4,
                                          four(dtk[:, c * HEADS:(c + 1) * HEADS]), ALU.mult)
                ins.then_inc(core["dve"], 1)
                for c in range(TC):
                    x4 = xtk[:, c, :].rearrange("p (h n) -> p h n", n=64)
                    ins = V.tensor_tensor(xde[:, c, :].rearrange("p (h n) -> p h n", n=64), x4,
                                          four(dend[:, c * HEADS:(c + 1) * HEADS]), ALU.mult)
                ins.then_inc(core["dve"], 1)
                for j in range(4):
                    dve.wait_ge(core["act"], act0 + (6, 9, 12, 14)[j])
                    for c in range(TC):
                        s = slice(c * P, (c + 1) * P)
                        ins = V.tensor_scalar(sg[j][:, s], mp[j % 2][:, s], col(acs, c * HEADS + 4 * g + j), 0.0,
                                              ALU.subtract, ALU.min)
                    ins.then_inc(core["dve"], 1)
                for j in range(4):
                    dve.wait_ge(core["act"], act0 + (8, 11, 13, 15)[j])
                    V.tensor_tensor(sg[j][:], sg[j][:], cbm.rearrange("p a b -> p (a b)"), ALU.mult).then_inc(core["dve"], 1)
                    V.tensor_tensor(cts[:, j, :], cg[b][:], ea[j][:], ALU.mult).then_inc(core["dve"], 1)
                dve.wait_ge(core["pe"], pe0 + 11)
                V.tensor_copy(st[0][:], mp[2][:, 0:256]).then_inc(core["dve"], 1)
                for c in (1, 2):
                    dve.wait_ge(core["dve"], (g + 1) * GPER["dve"] + 15 + c)
                    for j in range(4):
                        s = slice(64 * j, 64 * j + 64)
                        new = mp[2][:, 256 + 64 * j:256 + 64 * j + 64] if c == 1 else mp[3][:, s]
                        ins = V.scalar_tensor_tensor(st[c][:, s], st[c - 1][:, s], ea[j][:, c * P + P - 1:c * P + P], new,
                                                     ALU.mult, ALU.add)
                    ins.then_inc(core["dve"], 1)
                feed()
                for ct in range(2):
                    dve.wait_ge(core["pe"], pe0 + 12 + ct)
                    V.scalar_tensor_tensor(at(yT, 2 * g + ct), xg[b][:, ct, :], col(dskc, 2 * g + ct), mp[ct][:],
                                           ALU.mult, ALU.add).then_inc(core["dve"], 1)

            def cols_of(ap, h0):
                return cols(ap, h0, 4).unsqueeze(2).broadcast_to([P, 4, 64])

            dve.nop().then_inc(conv_ready, NBANK)
            tiles.inc(NPB_TILES + NK)
            phase_end(dve, "dve", ph)
            nstat.inc()
            norm_scale(NK, hT, uT, lambda k: pc("norm_mix", k))
            phase_end(dve, "dve", ph)
            dve.wait_ge(misc_in, 16 * 5)
            dve.wait_ge(stat_ready, nstat.v + 1)
            nstat.inc()
            for c in range(TC):
                s = slice(c * HEADS, (c + 1) * HEADS)
                ins = V.tensor_tensor(dtx[:, s], mp[0][:, s], dtb, ALU.add)
            link(ins)
            link(V.tensor_scalar(dA, dtx, -1.0, None, ALU.mult))
            V.tensor_tensor(dA, dtx, dA, ALU.min).then_inc(negabs_ready, 1)
            link(V.tensor_scalar(dtx, dtx, 0.0, None, ALU.max))
            dve.wait_ge(softplus_ready, 1)
            link(V.tensor_tensor(dtk, dtk, dtx, ALU.add))
            link(V.tensor_scalar(alog, alog, -1.0, None, ALU.mult))
            for c in range(TC):
                s = slice(c * HEADS, (c + 1) * HEADS)
                ins = V.tensor_tensor(dA[:, s], dtk[:, s], alog, ALU.mult)
            ins.then_inc(dA_ready, 1)
            dve.wait_ge(stat_ready, nstat.v + 1)
            nstat.inc()
            link(V.tensor_copy(acs, mp[1][:, 0:P]))
            V.tensor_copy(acsT[0:HEADS, :], mp[3][0:HEADS, :])
            V.tensor_tensor(dend, mp[2][:, 0:P], acs, ALU.subtract).then_inc(dend_ready, 1)
            dve.wait_ge(softplus_ready, 2)
            V.tensor_tensor(dend, dend, dtk, ALU.mult)
            phase_end(dve, "dve", ph)
            dve.nop().then_inc(core["dve"], GPER["dve"])
            conv_group(0)
            with dve.Fori(0, 3) as i:
                tiles.enter(i, 8), nconv.enter(i, 8), nsilu.enter(i, 8)
                chain.enter(i, 24)
                ssd_group(2 * i, 0, lambda: conv_group(2 * i + 1))
                ssd_group(2 * i + 1, 1, lambda: conv_group(2 * i + 2))
            tiles.leave(3), nconv.leave(3), nsilu.leave(3), chain.leave(3)
            ssd_group(6, 0, lambda: conv_group(7))
            ssd_group(7, 1, lambda: None)
            phase_end(dve, "dve", ph)
            split_both(whi, NK, 512, u_lo, u_hi)
            for m in range(16):
                if m % 4 == 2:
                    split_weight(whi, *((NK, 512) if m < 12 else (16, 256)))
                dve.wait_ge(tile_evac, tiles.v + 1)
                r = raw[tiles.s % NBANK][:, PAD:PAD + T]
                V.tensor_tensor(yT[:, m, :], yT[:, m, :], r, ALU.mult).then_inc(conv_ready, 1)
                tiles.inc()
                nconv.inc()
            phase_end(dve, "dve", ph)
            norm_scale(16, yT, yT, lambda k: pc("a_norm", k))
            phase_end(dve, "dve", ph)
            split_x(y_lo, yhi, range(16))
            for m in range(NK):
                residual(m)
                if m % 2 == 0:
                    split_weight(whi, *((16, 256) if m < 6 else (NK, 512)))
            phase_end(dve, "dve", ph)

            def ffn(layer):
                nstat.inc()
                norm_scale(NK, hT, uT, lambda k: pc("norm_ffn", layer * NK + k))
                phase_end(dve, "dve", ph)

                def pair(p, b):
                    for half in range(2):
                        c = p + FFN_TILES * half
                        if half == 0:
                            dve.wait_ge(silu_ready, NBANK + nsilu.v - 1)
                        convolve(3, lambda t: pc("f_conv_w", (layer * 3 + t) * 2 * FFN_TILES + c),
                                 pc("f_conv_b", layer * 2 * FFN_TILES + c), acc[(2 * b + half) % NBANK][:])
                    dve.wait_ge(silu_ready, NBANK + nsilu.v + 1)
                    nsilu.inc()
                    nglu.inc()
                    dve.wait_ge(conv_ready, NBANK + nconv.v)
                    V.tensor_tensor(at(ffa, p), sgate[b % 2][:], acc[(2 * b + 1) % NBANK][:], ALU.mult).then_inc(glu_ready, 1)

                split_x(u_lo, u_hi, range(NK))
                with dve.Fori(0, 5) as i:
                    tiles.enter(i, 8), nconv.enter(i, 8), nsilu.enter(i, 4), chain.enter(i, 16), nglu.enter(i, 4)
                    slots.enter(i, 2), nw.enter(i, 4)
                    for p in range(4):
                        pair(4 * i + p, p)
                        if p % 2 == 0:
                            split_weight(whi, NK, 512)
                tiles.leave(5), nconv.leave(5), nsilu.leave(5), chain.leave(5), nglu.leave(5), slots.leave(5), nw.leave(5)
                for p in range(2):
                    pair(20 + p, p)
                phase_end(dve, "dve", ph)
                split_both(wdhi, FFN_TILES, P, ff_lo, ffhi)
                for m in range(NK):
                    if m + 1 < NK:
                        split_weight(wdhi, FFN_TILES, P)
                    residual(m)
                phase_end(dve, "dve", ph)

            dve.nop().then_inc(glu_ready, 2)
            ffn(0)
            nstat.inc()
            norm_scale(NK, hT, uT, lambda k: pc("norm_mix", NK + k))
            for k in range(NK):
                V.memset(hg[:, k, 0:CONF_TAPS - 1], 0.0)
            phase_end(dve, "dve", ph)
            for j0 in range(0, NK, 2):
                pair = (j0, j0 + 1)
                for j in pair:
                    dve.wait_ge(tile_evac, tiles.v + 2)
                    tiles.inc(2)
                    V.tensor_tensor(hg[:, j, CONF_TAPS - 1:], glu_a[j % 2][:], glu_b[j % 2][:], ALU.mult).then_inc(glu_ready, 1)
                    nglu.inc()
                dve.wait_ge(glu_ready, 2 + nglu.v)
                for t in range(CONF_TAPS):
                    for j in pair:
                        x = hg[:, j, CONF_TAPS - 1 - t:CONF_TAPS - 1 - t + T]
                        w = pc("dw_w", (CONF_TAPS - 1 - t) * NK + j)
                        if t == 0:
                            ins = V.tensor_scalar(cv[:, j, :], x, w, pc("dw_b", j), ALU.mult, ALU.add)
                        else:
                            dve.wait_ge(dve_chain, chain.v - 1)
                            ins = V.scalar_tensor_tensor(cv[:, j, :], x, w, cv[:, j, :], ALU.mult, ALU.add)
                        ins.then_inc(dve_chain, 1)
                        chain.inc()
            phase_end(dve, "dve", ph)
            slots.inc(4)
            split_weight(whi, NK, 512)
            layer_norm(NK, cv, xc, lambda k: pc("ln_g", k))
            phase_end(dve, "dve", ph)
            split_x(u_lo, u_hi, range(NK))
            for m in range(NK):
                residual(m)
                if m % 4 == 1:
                    split_weight(whi, NK, 512)
            phase_end(dve, "dve", ph)
            ffn(1)
            nstat.inc()
            norm_scale(NK, hT, hT, lambda k: pc("norm_final", k))
            phase_end(dve, "dve", ph)
            tiles.inc(4 + 2 + 20)

            def reduce_angle(r, a, n, shift):
                link(V.tensor_scalar(n, a, 1.0 / TWO_PI, shift, ALU.mult, ALU.add))
                link(V.tensor_scalar(n, n, ROUND, ROUND, ALU.add, ALU.subtract))
                link(V.scalar_tensor_tensor(r, n, -TWO_PI_HI, a, ALU.mult, ALU.add))
                link(V.scalar_tensor_tensor(r, n, -TWO_PI_LO, r, ALU.mult, ALU.add))
                if shift:
                    link(V.tensor_scalar(r, r, shift * TWO_PI, None, ALU.add))
                return V.tensor_scalar(r, r, PI_BELOW, -PI_BELOW, ALU.min, ALU.max)

            rot = slice(64, 96)
            split_both(whi, NK, 512, h_lo, u_hi)
            dve.wait_ge(in2, 16 * 5)
            link(V.tensor_copy(ang[rot, :], posi[rot, :]))
            link(V.tensor_scalar(ang[rot, :], ang[rot, :], sc_consts[rot, 0:1], None, ALU.mult))
            for _ in range(5):
                split_weight(whi, NK, 512)
            phase_end(dve, "dve", ph)
            nstat.inc()
            norm_scale(2, hq, hq, lambda k: pc("q_norm_g", k))
            reduce_angle(sinT[rot, :], ang[rot, :], turns[rot, :], 0.0).then_inc(ang_ready, 1)
            reduce_angle(cosT[rot, :], ang[rot, :], turns[rot, :], 0.25).then_inc(ang_ready, 1)
            dve.wait_ge(sin_ready, 2)
            link(V.tensor_scalar(sinT[rot, :], sinT[rot, :], sc_consts[rot, 1:2], None, ALU.mult))
            link(V.tensor_tensor(kro[rot, :], kro[rot, :], cosT[rot, :], ALU.mult))
            link(V.tensor_tensor(krr[rot, :], krr[rot, :], sinT[rot, :], ALU.mult))
            V.tensor_tensor(kro[rot, :], kro[rot, :], krr[rot, :], ALU.add)
            phase_end(dve, "dve", ph)
            nstat.inc()
            norm_scale(2, hkv, hkv, lambda k: pc("kv_norm_g", k))
            link(V.tensor_scalar(negm, stri[:], -1e30, None, ALU.mult))
            phase_end(dve, "dve", ph)

            def head_rope(h):
                b = h % 2
                tiles.inc(4)
                dve.wait_ge(sin_ready, 2 + h + 1)
                link(V.tensor_tensor(qh[b][rot, :], qh[b][rot, :], cosT[rot, :], ALU.mult))
                link(V.tensor_tensor(rq[rot, :], rq[rot, :], sinT[rot, :], ALU.mult))
                V.tensor_tensor(qh[b][rot, :], qh[b][rot, :], rq[rot, :], ALU.add).then_inc(head_q, 1)

            def attention(s, n_items, per_head, blocks, causal, scale, probs, mx, nmx, rsm, rrc, out_tile, after):
                for n in range(n_items + 1):
                    if n < n_items:
                        nb = blocks(n)
                        dve.wait_ge(s["scores"], n + 1)
                        if n >= 3:
                            dve.wait_ge(s["turned"], n - 2)
                        p = probs[n % 3]
                        bank = mp[n % 2]
                        if causal:
                            if nb > 1:
                                V.tensor_copy(p[:, 0:(nb - 1) * P], bank[:, 0:(nb - 1) * P])
                            link(V.tensor_tensor(p[:, (nb - 1) * P:nb * P], bank[:, (nb - 1) * P:nb * P], negm, ALU.add))
                        else:
                            link(V.tensor_copy(p[:, 0:nb * P], bank[:, 0:nb * P]))
                        link(V.tensor_reduce(mx[:, n:n + 1], p[:, 0:nb * P], AX.X, ALU.max))
                        V.tensor_scalar(nmx[:, n:n + 1], mx[:, n:n + 1], -scale, None, ALU.mult).then_inc(s["masked"], 1)
                        after(n)
                    m = n - 1
                    if 0 <= m < n_items:
                        dve.wait_ge(s["exped"], m + 1)
                        link(V.reciprocal(rrc[:, m:m + 1], rsm[:, m:m + 1]))
                        p = probs[m % 3][:, 0:blocks(m) * P]
                        V.tensor_scalar(p, p, rrc[:, m:m + 1], None, ALU.mult).then_inc(s["normed"], 1)
                    m = n - 4
                    if m >= 0 and m % per_head == per_head - 1 and m < n_items - 1:
                        dve.wait_ge(s["pv"], m + 1)
                        V.tensor_copy(out_tile(m // per_head), mp[3][:]).then_inc(s["out"], 1)
                dve.wait_ge(s["pv"], n_items)
                V.tensor_copy(out_tile(n_items // per_head - 1), mp[3][:]).then_inc(s["out"], 1)

            head_rope(0)
            attention(att[0], 32, 8, lambda n: n % TC + 1, True, MLA_SCALE, pb, smax, nmax, rsum, rrec,
                      lambda k: attnT[:, k, :],
                      lambda n: head_rope(n // TC + 1) if n % TC == 3 and n // TC < 7 else None)
            phase_end(dve, "dve", ph)
            for m in range(NK):
                r = raw[tiles.s % NBANK][:, PAD:PAD + T]
                dve.wait_ge(tile_evac, tiles.v + 1)
                V.tensor_tensor(gm[:, m, :], gm[:, m, :], r, ALU.mult).then_inc(conv_ready, 1)
                tiles.inc()
                nconv.inc()
            phase_end(dve, "dve", ph)
            S = lambda k: s5p[:, k, :]
            are, aim = pcols("s5_a_re", 0, S5T), pcols("s5_a_im", 0, S5T)
            dve.wait_ge(in3, 16 * 8)
            dve.wait_ge(s5_a, 1)
            V.tensor_tensor(S(1), are, S(0), ALU.mult).then_inc(s5_cat, 1)
            link(V.tensor_tensor(S(2), aim, S(0), ALU.mult))
            link(reduce_angle(S(3), S(2), S(6), 0.0))
            link(V.tensor_scalar(S(5), S(3), 1.0 / TWO_PI, None, ALU.mult))
            reduce_angle(S(4), S(2), S(6), 0.25).then_inc(s5_cat, 1)
            dve.wait_ge(s5_a, 3)
            link(V.tensor_tensor(S(7), S(1), S(4), ALU.mult))
            link(V.tensor_scalar(S(7), S(7), -1.0, None, ALU.add))
            link(V.tensor_tensor(S(8), S(1), S(3), ALU.mult))
            link(V.tensor_tensor(S(9), are, are, ALU.mult))
            link(V.tensor_tensor(S(10), aim, aim, ALU.mult))
            link(V.tensor_tensor(S(9), S(9), S(10), ALU.add))
            link(V.reciprocal(S(9), S(9)))
            link(V.tensor_tensor(S(10), S(7), are, ALU.mult))
            link(V.tensor_tensor(S(11), S(8), aim, ALU.mult))
            link(V.tensor_tensor(S(10), S(10), S(11), ALU.add))
            link(V.tensor_tensor(S(10), S(10), S(9), ALU.mult))
            link(V.tensor_tensor(S(11), S(8), are, ALU.mult))
            link(V.tensor_tensor(S(12), S(7), aim, ALU.mult))
            link(V.tensor_tensor(S(11), S(11), S(12), ALU.subtract))
            link(V.tensor_tensor(S(11), S(11), S(9), ALU.mult))
            V.memset(bda, 0.0)
            link(V.memset(bdb, 0.0))
            wide = lambda k: S(k).unsqueeze(2).broadcast_to([P, S5T, 16])
            for dst, a, b, op in ((bda, bre, bim, ALU.subtract), (bdb, bim, bre, ALU.add)):
                link(V.tensor_tensor(btmp, b, wide(11), ALU.mult))
                link(V.tensor_tensor(y5.rearrange("p (a b) -> p a b", b=32)[:, :, 0:16], a, wide(10), ALU.mult))
                for two in range(2):
                    half = slice(64 * two, 64 * two + 64)
                    link(V.tensor_tensor(dst[half, :, 16 * two:16 * two + 16],
                                         y5.rearrange("p (a b) -> p a b", b=32)[half, :, 0:16], btmp[half, :, :], op))
            for n in range(2):
                for two in range(2):
                    V.tensor_scalar(cbig[:, n, :, 64 * two:64 * two + 64], craw[:, n, :, :], sc_consts[:, 2 + two:3 + two],
                                    None, ALU.mult)
            phase_end(dve, "dve", ph)
            tiles.inc(5)
            phase_end(dve, "dve", ph)

            def phases(j):
                dsts = ((st5[j % 2], 0.0), (ct5[j % 2], 0.25))
                for n, (dst, shift) in enumerate(dsts):
                    ins = V.tensor_scalar(wtb[n], iot, S(5)[:, j:j + 1], shift, ALU.mult, ALU.add)
                yield ins
                for n, (dst, shift) in enumerate(dsts):
                    ins = V.tensor_scalar(dst, wtb[n], ROUND, ROUND, ALU.add, ALU.subtract)
                yield ins
                for n, (dst, shift) in enumerate(dsts):
                    ins = V.tensor_tensor(dst, wtb[n], dst, ALU.subtract).then_inc(s5_ph, 1)
                yield ins

            steps = phases(0)
            link(next(steps))
            link(next(steps))
            next(steps)
            for j in range(S5T):
                b = j % 2
                c, s_ = ct5[b], st5[b]
                steps = phases(j + 1) if j + 1 < S5T else None
                dve.wait_ge(sin_ready, 2 + 8 + 2 * j + 2)
                dve.wait_ge(tile_evac, tiles.v + 2)
                tiles.inc(2)
                V.tensor_tensor(zr[0], c, acc[0][:], ALU.mult)
                V.tensor_tensor(y5, s_, acc[1][:], ALU.mult)
                V.tensor_tensor(t5, s_, acc[0][:], ALU.mult)
                V.tensor_tensor(zr[1], c, acc[1][:], ALU.mult).then_inc(s5_b, 1)
                dve.wait_ge(s5_b, j + 1)
                V.tensor_tensor(zr[0], zr[0], y5, ALU.add)
                ins = V.tensor_tensor(zr[1], zr[1], t5, ALU.subtract)
                if steps:
                    ins = next(steps)
                link(ins)
                mag = S(1)[:, j:j + 1].broadcast_to([P, T])
                V.tensor_tensor_scan(zi[0], mag, zr[0], 0.0, ALU.mult, ALU.add)
                ins = V.tensor_tensor_scan(zi[1], mag, zr[1], 0.0, ALU.mult, ALU.add)
                if steps:
                    ins = next(steps)
                link(ins)
                for n, (a, z) in enumerate(((c, zi[0]), (s_, zi[1]), (s_, zi[0]), (c, zi[1]))):
                    if j >= 1:
                        dve.wait_ge(s5_yd, 4 * (j - 1) + n + 1)
                    V.tensor_tensor(pr5[n], a, z, ALU.mult).then_inc(s5_c, 1)
                if steps:
                    next(steps)
            phase_end(dve, "dve", ph)
            for q in range(4):
                V.scalar_tensor_tensor(us[:, q, :], us[:, q, :], pc("s5_d", q), mp[q][:], ALU.mult, ALU.add).then_inc(s5_cat, 1)
            phase_end(dve, "dve", ph)
            slots.inc()
            split_both(wdhi, 4, 1024, us_lo, us_hi)
            for m in range(NK):
                dve.wait_ge(tile_evac, tiles.v + 2)
                tiles.inc()
                r = raw[tiles.s % NBANK][:, PAD:PAD + T]
                tiles.inc()
                nconv.inc()
                nglu.inc()
                b = zr[m % 2]
                link(V.tensor_tensor(b, b, r, ALU.mult))
                dve.nop().then_inc(conv_ready, 1)
                link(V.tensor_tensor(b, b, gs[:, m, :], ALU.mult))
                V.tensor_tensor(gm[:, m, :], gm[:, m, :], b, ALU.add).then_inc(glu_ready, 1)
                if m % 4 == 1:
                    split_weight(wdhi, *((4, 1024) if m < 4 else (NK, 512)))
            phase_end(dve, "dve", ph)
            split_x(gm_lo, gm_hi, range(NK))
            for m in range(NK):
                residual(m, ALPHA)
                if m == 1:
                    split_weight(wdhi, NK, 512)
            phase_end(dve, "dve", ph)
            layer_norm(NK, hT, xc, lambda k: pc("ln1_g", k))
            phase_end(dve, "dve", ph)
            tiles.inc(NK)
            phase_end(dve, "dve", ph)
            layer_norm(NK, memT, memc, lambda k: pc("mem_ln_g", k), n=256)
            phase_end(dve, "dve", ph)
            tiles.inc(10)
            phase_end(dve, "dve", ph)
            attention(att[1], 16, 4, lambda n: 2, False, X_SCALE, xpb, xsm[0], xsm[1], xsm[2], xsm[3],
                      lambda k: ox[:, k, :], lambda n: None)
            phase_end(dve, "dve", ph)
            for m in range(NK):
                residual(m, ALPHA)
            phase_end(dve, "dve", ph)
            layer_norm(NK, hT, xc, lambda k: pc("ln2_g", k))
            phase_end(dve, "dve", ph)
            dve.wait_ge(rt["scores"], 1)
            dve.wait_ge(in3, 16 * 12)
            c4 = lambda ap: ap.rearrange("p (c e) -> p c e", e=NE)
            link(V.tensor_tensor(c4(sel), c4(scr), rbias.unsqueeze(1).broadcast_to([P, TC, NE]), ALU.add))
            for g in range(TC * 8):
                ins = V.max(m8[:, g, :], sel[:, 8 * g:8 * g + 8])
            link(ins)
            gflat = gsc.rearrange("p c g -> p (c g)")
            link(V.tensor_tensor(gflat.unsqueeze(2), m8[:, :, 0:1], m8[:, :, 1:2], ALU.add))
            by_j = gsc.unsqueeze(2).broadcast_to([P, TC, 8, 8])
            by_i = gsc.unsqueeze(3).broadcast_to([P, TC, 8, 8])
            v4 = lambda ap: ap.rearrange("p (c i) j -> p c i j", c=TC)
            V.tensor_tensor(v4(gpair), by_j, by_i, ALU.is_gt)
            link(V.tensor_tensor(v4(geq), by_j, by_i, ALU.is_equal))
            lower = sc_c2[:, 4:68].rearrange("p (i j) -> p i j", j=8).unsqueeze(1).broadcast_to([P, TC, 8, 8])
            link(V.tensor_tensor(v4(geq), v4(geq), lower, ALU.mult))
            link(V.tensor_tensor(gpair, gpair, geq, ALU.add))
            gm_flat = gmask.rearrange("p c g -> p (c g)")
            link(V.tensor_reduce(gm_flat, gpair, AX.X, ALU.add))
            link(V.tensor_scalar(gm_flat, gm_flat, 4.0, None, ALU.is_lt))
            link(V.tensor_scalar(gflat, gm_flat, -1.0, 1e30, ALU.add, ALU.mult))
            e8 = lambda ap: ap.rearrange("p (g e) -> p g e", e=8)
            link(V.tensor_tensor(e8(sel), e8(sel), gm_flat.unsqueeze(2).broadcast_to([P, TC * 8, 8]), ALU.mult))
            link(V.tensor_tensor(e8(sel), e8(sel), gflat.unsqueeze(2).broadcast_to([P, TC * 8, 8]), ALU.add))
            for c in range(TC):
                ins = V.max(m8[:, c, :], sel[:, c * NE:(c + 1) * NE])
            link(ins)
            for c in range(TC):
                ins = V.match_replace(rtmp[:, c * NE:(c + 1) * NE], m8[:, c, :], sel[:, c * NE:(c + 1) * NE], -3e38)
            link(ins)
            link(V.tensor_tensor(mask, rtmp, sel, ALU.not_equal))
            link(V.tensor_tensor(rtmp, scr, mask, ALU.mult))
            link(V.tensor_reduce(rden, c4(rtmp), AX.X, ALU.add))
            link(V.reciprocal(rden, rden))
            link(V.tensor_tensor(c4(rtmp), c4(rtmp), rden.unsqueeze(2).broadcast_to([P, TC, NE]), ALU.mult))
            link(V.tensor_scalar(rinfo[:, :, 2:3], rtmp.unsqueeze(2), 2.5, None, ALU.mult))
            tiles.inc(8)
            for j in range(2):
                dve.wait_ge(tile_evac, tiles.v + 2)
                tiles.inc()
                r = raw[tiles.s % NBANK][:, PAD:PAD + T]
                tiles.inc()
                nconv.inc()
                nglu.inc()
                link(V.tensor_tensor(sact[:, j, :], ssil[j], r, ALU.mult))
                dve.nop().then_inc(conv_ready, 1)
                dve.nop().then_inc(glu_ready, 1)
            for m in range(NK):
                dve.wait_ge(tile_evac, tiles.v + 1)
                r = raw[tiles.s % NBANK][:, PAD:PAD + T]
                V.scalar_tensor_tensor(sq[:, m, :], hT[:, m, :], ALPHA, r, ALU.mult, ALU.add).then_inc(conv_ready, 1)
                tiles.inc()
                nconv.inc()
            assert nconv.s == CONVS
            tiles.inc(8)
            phase_end(dve, "dve", ph)
            dve.wait_ge(rt["pos"], 1)
            pflat = posm.rearrange("p c e -> p (c e)")
            link(V.scalar_tensor_tensor(pflat, mp[1][:, 0:TC * NE], 1.0, mask, ALU.add, ALU.mult))
            link(V.tensor_scalar(pflat, pflat, -1.0, None, ALU.add))
            link(V.tensor_reduce(cntf, mp[2][:, 0:NE], AX.X, ALU.max))
            link(V.tensor_copy(cnti, cntf))
            phase_end(dve, "dve", ph)

            def wait(s, x):
                if not (isinstance(x, int) and x <= 0):
                    dve.wait_ge(s, x)

            def m_onehot(e, n, b):
                wait(moe["idx"], n - 1)
                for c in range(TC):
                    ins = V.tensor_scalar(oneh[b][:, c, :], slotrow, col(pflat, c * NE + e), None, ALU.is_equal)
                ins.then_inc(moe["onehot"], 1)

            def m_conv(n, q, again=None):
                wait(moe["idx"], n + 1)
                wait(moe["scattered"], 16 * n - 48)
                ins = V.tensor_scalar(sidf[:, 0:1], mp[1][:, 1:2], slotcol[:, 1:2], slotcol[:, 0:1], ALU.mult, ALU.add)
                if again is None:
                    link(ins)
                else:
                    ins.then_inc(moe_again, 1)
                    dve.wait_ge(moe_again, again)
                V.tensor_copy(swt[q], mp[1][:, 2:3])
                V.tensor_tensor(sidx[q], sidf[:, 0:1], mp[1][:, 0:1], ALU.add).then_inc(moe["conv"], 1)
                wait(moe["conv"], n + 1)

            def m_act(n, b, q):
                wait(moe["silu"], n + 1)
                wait(moe["actturned"], n)
                V.scalar_tensor_tensor(actE, tp[b][:, 256:512], swt[q], silg, ALU.mult, ALU.mult).then_inc(moe["act"], 1)

            def m_y1(n, b):
                wait(moe["down"], n + 1)
                wait(moe["scattered"], 16 * n - 16)
                V.tensor_copy(ye[b][:, 512:1024], mp[3][:]).then_inc(moe["y1"], 1)

            def m_step(e, k):
                fixed = isinstance(e, int)
                m_act(e, k % 2, k)
                if not fixed or e + 2 < NE:
                    m_conv(e + 2, (k + 2) % 4)
                if not fixed or e + 3 < NE:
                    m_onehot(e + 3, e + 3, (k + 3) % 2)
                m_y1(e, k % 2)

            m_onehot(0, 0, 0)
            m_onehot(1, 1, 1)
            m_conv(0, 0)
            m_conv(1, 1)
            m_onehot(2, 2, 0)
            for e in range(4):
                m_step(e, e)
            with dve.Fori(0, NE // 4 - 2) as i:
                chain.enter(i, 4)
                for k in range(4):
                    m_step(4 * i + 4 + k, k)
            chain.leave(NE // 4 - 2)
            for e in range(NE - 4, NE):
                m_step(e, e % 4)
            phase_end(dve, "dve", ph)
            crowded = dve.value_load(cnti[0:1, 0:1])
            with dve.If(crowded > CAP):
                with dve.Fori(0, 3) as bb:
                    V.tensor_scalar(slotrow, slotrow, float(CAP), None, ALU.add).then_inc(moe_row, 1)
                    dve.wait_ge(moe_row, bb + 1)
                    dve.nop().then_inc(wait_taken, 1)
                    with dve.Fori(0, NE) as e:
                        n = NE * bb + e + NE
                        m_onehot(e, n, 0)
                        dve.wait_ge(moe["scattered"], NE * 16 * bb + 16 * e + 16 * NE)
                        m_conv(n, 0, again=NE * bb + e + 1)
                        m_act(n, 0, 0)
                        m_y1(n, 0)
            with dve.Else():
                dve.nop()
            phase_end(dve, "dve", ph)
            for c in range(TC):
                dve.wait_ge(fin_in, 16 * (3 + c))
                for half in range(2):
                    ins = V.bn_stats(bst[:, 2 * c + half, :], fin[c][:, 512 * half:512 * half + 512])
                link(ins)
                V.bn_aggr(mv[:, c, :], bst[:, 2 * c:2 * c + 2, :]).then_inc(var_ready, 1)
                dve.wait_ge(rs_ready, c + 1)
                link(V.reciprocal(rs3[:, c:c + 1], rs3[:, c:c + 1]))
                link(V.tensor_scalar(fin[c], fin[c], mv[:, c, 0:1], rs3[:, c:c + 1], ALU.subtract, ALU.mult))
                link(V.tensor_tensor(fin[c], fin[c], g3, ALU.mult))
                V.tensor_tensor(fin[c], fin[c], b3, ALU.add).then_inc(fin_ready, 1)
            phase_end(dve, "dve", ph)


def kernel(**inputs):
    import concourse.bacc as bacc
    from concourse.bass_utils import run_bass_kernel_spmd

    nc = bacc.Bacc("TRN2", target_bir_lowering=False, num_devices=1)
    arrays, aps = {}, {}
    given = {k: v for k, v in inputs.items() if k not in UNUSED}
    given.update(shape_constants())
    for name, a in given.items():
        a = np.ascontiguousarray(a)
        arrays["in_" + name] = a
        aps[name] = nc.dram_tensor("in_" + name, a.shape, mybir.dt.from_np(a.dtype), kind="ExternalInput").ap()
    out = nc.dram_tensor("out_dram", (1, T, D), F32, kind="ExternalOutput").ap()
    build(nc, aps, out)
    r = run_bass_kernel_spmd(nc, [arrays], core_ids=[0])
    return r.results[0]["out_dram"]
```
